# Optimizing a Trainium2 kernel written in Bass

```python
import jax
import jax.numpy as jnp
from jax import lax
import numpy as np

D_MODEL = 1024
BATCH = 1
SEQ = 128
DEPTH = 2
DEC_BATCH = 1
DEC_SEQ = 512
PAST_LEN = 128

GRID_W = 64
HEAD_DIM = 64
N_RET_HEADS = 8
N_NA_HEADS = 8
RET_WIDTH = N_RET_HEADS * HEAD_DIM
NA_WIDTH = N_NA_HEADS * HEAD_DIM
MIX_WIDTH = RET_WIDTH + NA_WIDTH
IN_WIDTH = 4 * RET_WIDTH + 3 * NA_WIDTH
D_FF = 2816
CONV_W = 3
CHUNK = 128
NA_KH_MAX = 8
NA_KW = 16
NA_QB = 16
NA_KB = 2 * NA_KW
ATTN_QBLOCK = 128
ROPE_BASE = 10000.0
EPS = 1e-6
NEG_INF = -1e9

kernel_name = "hymba_retention_natten_prefix_dit"

def _rmsnorm(x, g):
    xf = x.astype(jnp.float32)
    y = xf * lax.rsqrt(jnp.mean(xf * xf, axis=-1, keepdims=True) + EPS)
    return (y * g.astype(jnp.float32)).astype(x.dtype)

def _modulation(cond, ada_w, ada_b):
    m = jax.nn.silu(cond) @ ada_w + ada_b
    return jnp.split(m[:, None, :], 6, axis=-1)

def _split_proj(h, w_in):
    B, T, _ = h.shape
    p = h @ w_in
    cuts = [RET_WIDTH, 2 * RET_WIDTH, 3 * RET_WIDTH, 4 * RET_WIDTH,
            4 * RET_WIDTH + NA_WIDTH, 4 * RET_WIDTH + 2 * NA_WIDTH]
    rq, rk, rv, rg, nq, nk, nv = jnp.split(p, cuts, axis=-1)
    hr = lambda a: a.reshape(B, T, N_RET_HEADS, HEAD_DIM)
    hn = lambda a: a.reshape(B, T, N_NA_HEADS, HEAD_DIM)
    return hr(rq), hr(rk), hr(rv), rg, hn(nq), hn(nk), hn(nv)

def _rotate(x, pos):
    d = x.shape[-1]
    inv = jnp.power(ROPE_BASE, -jnp.arange(0, d, 2, dtype=jnp.float32) / d)
    ang = pos[:, None] * inv[None, :]
    cos = jnp.cos(ang)[None, :, None, :]
    sin = jnp.sin(ang)[None, :, None, :]
    xf = x.astype(jnp.float32)
    x1, x2 = xf[..., : d // 2], xf[..., d // 2:]
    return jnp.concatenate([x1 * cos - x2 * sin, x1 * sin + x2 * cos], axis=-1).astype(x.dtype)

def _rope_2d(x):
    T = x.shape[1]
    pos = jnp.arange(T)
    rows = (pos // GRID_W).astype(jnp.float32)
    cols = (pos % GRID_W).astype(jnp.float32)
    half = x.shape[-1] // 2
    return jnp.concatenate([_rotate(x[..., :half], rows), _rotate(x[..., half:], cols)], axis=-1)

def _retention_scan(q, k, v, log_gamma, s0):
    B, T, H, Dh = q.shape
    nc = T // CHUNK
    lg = log_gamma.astype(jnp.float32)
    pos = jnp.arange(CHUNK, dtype=jnp.float32)
    diff = pos[:, None] - pos[None, :]
    decay_in = jnp.where(diff >= 0, jnp.exp(lg[:, None, None] * jnp.maximum(diff, 0.0)), 0.0)
    q_dec = jnp.exp(lg[None, :] * (pos[:, None] + 1.0))
    k_dec = jnp.exp(lg[None, :] * (CHUNK - 1.0 - pos[:, None]))
    c_dec = jnp.exp(lg * CHUNK)

    def to_chunks(a):
        return a.astype(jnp.float32).reshape(B, nc, CHUNK, H, Dh).transpose(1, 0, 2, 3, 4)

    def step(s, qkv):
        qc, kc, vc = qkv
        scores = jnp.einsum('bihd,bjhd->bhij', qc, kc) * decay_in[None]
        inner = jnp.einsum('bhij,bjhe->bihe', scores, vc)
        cross = jnp.einsum('bihd,bhde->bihe', qc, s) * q_dec[None, :, :, None]
        s_new = s * c_dec[None, :, None, None] + jnp.einsum(
            'bjhd,bjhe->bhde', kc * k_dec[None, :, :, None], vc)
        return s_new, inner + cross

    s_fin, out = lax.scan(step, s0.astype(jnp.float32), (to_chunks(q), to_chunks(k), to_chunks(v)))
    out = out.transpose(1, 0, 2, 3, 4).reshape(B, T, H, Dh)
    return out, s_fin

def _bi_retention(q, k, v, g, lg_f, lg_b, s_f0, s_b0):
    B, T = q.shape[0], q.shape[1]
    q = q * (HEAD_DIM ** -0.5)
    o_f, s_f = _retention_scan(q, k, v, lg_f, s_f0)
    o_b, s_b = _retention_scan(jnp.flip(q, 1), jnp.flip(k, 1), jnp.flip(v, 1), lg_b, s_b0)
    o = o_f + jnp.flip(o_b, 1)
    mu = jnp.mean(o, axis=-1, keepdims=True)
    var = jnp.mean(jnp.square(o - mu), axis=-1, keepdims=True)
    o = ((o - mu) * lax.rsqrt(var + EPS)).reshape(B, T, RET_WIDTH).astype(g.dtype)
    return o * jax.nn.silu(g), s_f, s_b

def _context_attention(q, k, v):
    B, N, H, Dh = q.shape
    nb = N // ATTN_QBLOCK
    qb = q.reshape(B, nb, ATTN_QBLOCK, H, Dh).transpose(1, 0, 2, 3, 4)
    scale = HEAD_DIM ** -0.5

    def blk(qi):
        s = jnp.einsum('bqhd,bkhd->bhqk', qi, k).astype(jnp.float32) * scale
        p = jax.nn.softmax(s, axis=-1)
        return jnp.einsum('bhqk,bkhd->bqhd', p.astype(v.dtype), v)

    out = lax.map(blk, qb)
    return out.transpose(1, 0, 2, 3, 4).reshape(B, N, H * Dh)

def _neighbourhood_attention(q, k, v, ctx_k, ctx_v, rpb):
    B, T, H, Dh = q.shape
    rows = T // GRID_W
    kh = min(NA_KH_MAX, rows)
    ncb = GRID_W // NA_QB
    r = np.arange(rows)
    rs = np.clip(r - kh // 2, 0, rows - kh)
    row_idx = rs[:, None] + np.arange(kh)[None, :]
    dr_idx = row_idx - r[:, None] + NA_KH_MAX - 1
    jb = np.arange(ncb)
    kb = np.clip(jb * NA_QB - NA_KW // 2, 0, GRID_W - NA_KB)
    col_idx = kb[:, None] + np.arange(NA_KB)[None, :]
    qcol = jb[:, None] * NA_QB + np.arange(NA_QB)[None, :]
    cs = np.clip(qcol - NA_KW // 2, 0, GRID_W - NA_KW)
    col_ok = (col_idx[:, None, :] >= cs[:, :, None]) & (col_idx[:, None, :] < cs[:, :, None] + NA_KW)
    dc_idx = np.clip(col_idx[:, None, :] - qcol[:, :, None] + NA_KW - 1, 0, 2 * NA_KW - 2)
    L = kh * NA_KB
    scale = HEAD_DIM ** -0.5

    k_grid = k.reshape(B, rows, GRID_W, H, Dh)
    v_grid = v.reshape(B, rows, GRID_W, H, Dh)
    q_rows = q.reshape(B, rows, ncb, NA_QB, H, Dh).transpose(1, 0, 2, 3, 4, 5)
    rpb_f = rpb.astype(jnp.float32)

    def gather_rows(grid, ridx):
        g = grid[:, ridx][:, :, col_idx]
        return g.transpose(0, 2, 1, 3, 4, 5).reshape(B, ncb, L, H, Dh)

    def row_block(args):
        qr, ridx, dri = args
        kr = gather_rows(k_grid, ridx)
        vr = gather_rows(v_grid, ridx)
        bias = rpb_f[:, dri[None, None, :, None], dc_idx[:, :, None, :]]
        bias = jnp.where(col_ok[None, :, :, None, :], bias, NEG_INF).reshape(H, ncb, NA_QB, L)
        s_loc = jnp.einsum('bjqhd,bjlhd->bhjql', qr, kr).astype(jnp.float32) * scale + bias[None]
        s_ctx = jnp.einsum('bjqhd,bnhd->bhjqn', qr, ctx_k).astype(jnp.float32) * scale
        p = jax.nn.softmax(jnp.concatenate([s_loc, s_ctx], axis=-1), axis=-1)
        o = jnp.einsum('bhjql,bjlhd->bjqhd', p[..., :L].astype(vr.dtype), vr)
        o = o + jnp.einsum('bhjqn,bnhd->bjqhd', p[..., L:].astype(ctx_v.dtype), ctx_v)
        return o

    out = lax.map(row_block, (q_rows, jnp.asarray(row_idx, jnp.int32), jnp.asarray(dr_idx, jnp.int32)))
    return out.transpose(1, 0, 2, 3, 4, 5).reshape(B, T, H * Dh)

def _conv_ffn(h, w_up, conv_w, conv_b, w_down):
    T = h.shape[1]
    u = h @ w_up
    pad = CONV_W // 2
    up = jnp.pad(u, ((0, 0), (pad, pad), (0, 0)))
    u = sum(up[:, i:i + T] * conv_w[i] for i in range(CONV_W)) + conv_b
    a, gate = jnp.split(u, 2, axis=-1)
    return (jax.nn.silu(gate) * a) @ w_down

def _context_mixer(parts, lg_f, lg_b):
    rq, rk, rv, rg, nq, nk, nv = parts
    B = rq.shape[0]
    z = jnp.zeros((B, N_RET_HEADS, HEAD_DIM, HEAD_DIM), jnp.float32)
    ret, s_f, s_b = _bi_retention(rq, rk, rv, rg, lg_f, lg_b, z, z)
    na = _context_attention(nq, nk, nv)
    return jnp.concatenate([ret, na], axis=-1), (nk, nv, s_f, s_b)

def _latent_mixer(parts, lg_f, lg_b, rpb, ctx_k, ctx_v, s_f0, s_b0):
    rq, rk, rv, rg, nq, nk, nv = parts
    rq = _rope_2d(rq)
    rk = _rope_2d(rk)
    ret, _, _ = _bi_retention(rq, rk, rv, rg, lg_f, lg_b, s_f0, s_b0)
    na = _neighbourhood_attention(nq, nk, nv, ctx_k, ctx_v, rpb)
    return jnp.concatenate([ret, na], axis=-1), None

def _layer(x, cond, mixer, ada_w, ada_b, g_pre_mix, g_post_mix, g_pre_ffn, g_post_ffn,
           w_in, w_out, w_up, conv_w, conv_b, w_down):
    sh1, sc1, ga1, sh2, sc2, ga2 = _modulation(cond, ada_w, ada_b)
    h = _rmsnorm(x, g_pre_mix) * (1.0 + sc1) + sh1
    mixed, side = mixer(_split_proj(h, w_in))
    x = x + ga1 * _rmsnorm(mixed @ w_out, g_post_mix)
    h = _rmsnorm(x, g_pre_ffn) * (1.0 + sc2) + sh2
    x = x + ga2 * _rmsnorm(_conv_ffn(h, w_up, conv_w, conv_b, w_down), g_post_ffn)
    return x, side

def setup_inputs(seed: int = 0) -> dict:
    key = jax.random.key(seed)
    ks = jax.random.split(key, 24)
    f32 = jnp.float32

    def nrm(k, shape, scale):
        return scale * jax.random.normal(k, shape, f32)

    decay_base = jnp.log(jnp.power(2.0, 5.0 + jnp.arange(N_RET_HEADS, dtype=f32)) - 1.0)
    return {
        'x_prompt': nrm(ks[0], (BATCH, SEQ, D_MODEL), 1.0),
        'x_sample': nrm(ks[1], (DEC_BATCH, DEC_SEQ, D_MODEL), 1.0),
        'c': nrm(ks[2], (DEC_BATCH, D_MODEL), 1.0),
        'cache_na_k': nrm(ks[3], (DEC_BATCH, DEPTH, PAST_LEN, N_NA_HEADS, HEAD_DIM), 1.0),
        'cache_na_v': nrm(ks[4], (DEC_BATCH, DEPTH, PAST_LEN, N_NA_HEADS, HEAD_DIM), 1.0),
        'state_ret_fwd': nrm(ks[5], (DEC_BATCH, DEPTH, N_RET_HEADS, HEAD_DIM, HEAD_DIM), 0.5),
        'state_ret_bwd': nrm(ks[6], (DEC_BATCH, DEPTH, N_RET_HEADS, HEAD_DIM, HEAD_DIM), 0.5),
        'c_ctx': nrm(ks[7], (D_MODEL,), 1.0),
        'ada_w': nrm(ks[8], (DEPTH, D_MODEL, 6 * D_MODEL), 0.5 * D_MODEL ** -0.5),
        'ada_b': nrm(ks[9], (DEPTH, 6 * D_MODEL), 0.02),
        'g_pre_mix': 1.0 + nrm(ks[10], (DEPTH, D_MODEL), 0.05),
        'g_post_mix': 1.0 + nrm(ks[11], (DEPTH, D_MODEL), 0.05),
        'g_pre_ffn': 1.0 + nrm(ks[12], (DEPTH, D_MODEL), 0.05),
        'g_post_ffn': 1.0 + nrm(ks[13], (DEPTH, D_MODEL), 0.05),
        'w_in': nrm(ks[14], (DEPTH, D_MODEL, IN_WIDTH), D_MODEL ** -0.5),
        'ret_decay_fwd': decay_base + nrm(ks[15], (DEPTH, N_RET_HEADS), 0.1),
        'ret_decay_bwd': decay_base + nrm(ks[16], (DEPTH, N_RET_HEADS), 0.1),
        'na_rpb': nrm(ks[17], (DEPTH, N_NA_HEADS, 2 * NA_KH_MAX - 1, 2 * NA_KW - 1), 0.5),
        'w_out': nrm(ks[18], (DEPTH, MIX_WIDTH, D_MODEL), MIX_WIDTH ** -0.5),
        'w_up': nrm(ks[19], (DEPTH, D_MODEL, 2 * D_FF), D_MODEL ** -0.5),
        'conv_w': nrm(ks[20], (DEPTH, CONV_W, 2 * D_FF), CONV_W ** -0.5),
        'conv_b': nrm(ks[21], (DEPTH, 2 * D_FF), 0.02),
        'w_down': nrm(ks[22], (DEPTH, D_FF, D_MODEL), D_FF ** -0.5),
    }

def reference(x_prompt, x_sample, c, cache_na_k, cache_na_v, state_ret_fwd, state_ret_bwd, c_ctx,
              ada_w, ada_b, g_pre_mix, g_post_mix, g_pre_ffn, g_post_ffn, w_in,
              ret_decay_fwd, ret_decay_bwd, na_rpb, w_out, w_up, conv_w, conv_b, w_down):
    y_p = x_prompt
    ks_, vs_, sfs_, sbs_ = [], [], [], []
    for l in range(DEPTH):
        lg_f = jax.nn.log_sigmoid(ret_decay_fwd[l].astype(jnp.float32))
        lg_b = jax.nn.log_sigmoid(ret_decay_bwd[l].astype(jnp.float32))
        mixer = lambda parts, lg_f=lg_f, lg_b=lg_b: _context_mixer(parts, lg_f, lg_b)
        y_p, (k_l, v_l, sf_l, sb_l) = _layer(
            y_p, c_ctx[None, :], mixer, ada_w[l], ada_b[l], g_pre_mix[l], g_post_mix[l],
            g_pre_ffn[l], g_post_ffn[l], w_in[l], w_out[l], w_up[l], conv_w[l], conv_b[l], w_down[l])
        ks_.append(k_l)
        vs_.append(v_l)
        sfs_.append(sf_l.astype(x_prompt.dtype))
        sbs_.append(sb_l.astype(x_prompt.dtype))

    y_s = x_sample
    for l in range(DEPTH):
        lg_f = jax.nn.log_sigmoid(ret_decay_fwd[l].astype(jnp.float32))
        lg_b = jax.nn.log_sigmoid(ret_decay_bwd[l].astype(jnp.float32))
        mixer = (lambda parts, lg_f=lg_f, lg_b=lg_b, rpb=na_rpb[l], ck=cache_na_k[:, l], cv=cache_na_v[:, l],
                 sf0=state_ret_fwd[:, l], sb0=state_ret_bwd[:, l]:
                 _latent_mixer(parts, lg_f, lg_b, rpb, ck, cv, sf0, sb0))
        y_s, _ = _layer(
            y_s, c, mixer, ada_w[l], ada_b[l], g_pre_mix[l], g_post_mix[l],
            g_pre_ffn[l], g_post_ffn[l], w_in[l], w_out[l], w_up[l], conv_w[l], conv_b[l], w_down[l])

    new_na_k = jnp.stack(ks_, axis=1)
    new_na_v = jnp.stack(vs_, axis=1)
    new_ret_fwd = jnp.stack(sfs_, axis=1)
    new_ret_bwd = jnp.stack(sbs_, axis=1)
    return (y_p, y_s, new_na_k, new_na_v, new_ret_fwd, new_ret_bwd)


_drawn_inputs = setup_inputs


def setup_inputs(seed=0):
    import zlib

    import numpy as np

    out = dict(_drawn_inputs(seed))
    spreads = {}
    factors = {'state_ret_fwd': 8.0, 'state_ret_bwd': 8.0, 'conv_b': 5.187}
    for name, (base, spread) in spreads.items():
        noise = np.random.default_rng([zlib.crc32(name.encode()), seed]).standard_normal(out[name].shape)
        drawn = base * np.exp(spread * noise) if base else spread * noise
        out[name] = jnp.asarray(drawn.astype(out[name].dtype))
    for name, factor in factors.items():
        out[name] = (out[name] * factor).astype(out[name].dtype)
    return out
```

```python
from contextlib import ExitStack

import numpy as np

import concourse.bass as bass
from concourse import mybir

F32 = mybir.dt.float32
F32R = mybir.dt.float32r
ACT = mybir.ActivationFunctionType
ALU = mybir.AluOpType
AX = mybir.AxisListType

P = 128
D = 1024
DEPTH = 2
CTX = 128
LAT = 512
TOK = CTX + LAT
NT = TOK // P
GRID_W = 64
ROWS = LAT // GRID_W
DH = 64
H = 8
HP = H // 2
F = 2816
KD = D // P
KF = F // P
W = 512
NB_IN = 7
W_IN_COL = [0, 1, 2, 3, 6, 4, 5]
EPS = 1e-6
NEG = -1e9
BIG = 3.0e38
SCALE = DH ** -0.5
CB = 16
NQB = GRID_W // CB
DIST = 7 * P

SLOTS = 4
ADA = 6 * KD
ADA_FIRST = 20
G_IN = NB_IN * 4
G_OUT = 2 * 4
G_UP = 2 * KF
DOWN_KT = [(2 * i, 2 * i + 1) for i in range(10)] + [(20,), (21,)]
G_DOWN = 2 * len(DOWN_KT)
GW = G_IN + G_OUT + G_UP + G_DOWN
GS = ADA + GW
ROUNDS = GS // SLOTS
W_OUT0 = G_IN
W_UP0 = W_OUT0 + G_OUT
W_DOWN0 = W_UP0 + G_UP
S_IN0 = ADA_FIRST
S_OUT0 = S_IN0 + NB_IN * 8
S_UP0 = S_OUT0 + G_OUT
S_DOWN0 = S_UP0 + G_UP
assert GS % SLOTS == 0 and GW % SLOTS == 0 and S_DOWN0 + G_DOWN == GS


def stream_in(b, q):
    return S_IN0 + 8 * b + (q if q < 2 else q + 2)


def stream_ada(b, q):
    return S_IN0 + 8 * b + (q + 2 if q < 2 else q + 4)


C_TAP, C_CB, C_AB, C_GM, C_GF, C_PM, C_PF = 0, 132, 176, 224, 232, 240, 248
NPAR = 256

UNITS = [(jb, h) for jb in range(NQB + 1) for h in range(H)]
NBIAS = 5


def key_blocks(jb):
    if jb == NQB:
        return [], 0
    if jb == 0:
        return [1, 0], 3
    if jb == NQB - 1:
        return [NQB - 1, NQB - 2], 0
    return [jb - 1, jb, jb + 1], 1


def build(nc, t):
    with ExitStack() as ctx:
        def sem(name):
            return ctx.enter_context(nc.semaphore(name))

        def sb(name, shape, dt=F32, stack=ctx):
            return stack.enter_context(nc.sbuf_tensor(name, shape, dt))

        x = sb("x", [P, NT, D])
        raw = sb("raw", [P, SLOTS, 1024])
        w_hi = sb("w_hi", [P, SLOTS, 1024], F32R)
        w_lo = sb("w_lo", [P, SLOTS, 1024], F32R)
        ident = sb("ident", [P, P])
        rope = sb("rope", [P, 2, NT - 1, DH])
        dist = sb("dist", [P, DIST])
        qpos = sb("qpos", [P, 2, LAT])
        kpos = sb("kpos", [P, 2])
        masks = sb("masks", [P, NBIAS, CB])
        cond = sb("cond", [P, 2, KD])
        par = sb("par", [P, NPAR])
        mod = sb("mod", [P, ADA, 2])
        gain = sb("gain", [P, KD, 2])
        dec = sb("dec", [P, 2, H])
        lgt = sb("lgt", [P, 4, 2 * H])
        lg = sb("lg", [P, 2, H])
        nlg = sb("nlg", [P, H])
        lgp = sb("lgp", [P, 2, HP])
        kdec = sb("kdec", [P, 2, H])
        st0 = sb("st0", [P, 2, HP, DH])
        ctx_kT = sb("ctx_kT", [P, HP, P])
        ctx_v = sb("ctx_v", [P, H, DH + 1])
        ssq = sb("ssq", [P, 2, NT])
        base = sb("base", [P, NT])
        std = sb("std", [P, NT])
        sq = sb("sq", [P, D])
        rstd = sb("rstd", [P, NT])
        eps = sb("eps", [P, 1])
        prime = sb("prime", [P, 16])
        gn = sb("gn", [P, 4, NT, H])
        nmax = sb("nmax", [P, 4])
        cmax = sb("cmax", [P, 4, 2])
        rec = sb("rec", [P, 2, 4])

        with ExitStack() as s:
            m_hi = sb("m_hi", [P, 4, TOK], F32R, s)
            m_lo = sb("m_lo", [P, 4, TOK], F32R, s)
        aT_hi = sb("aT_hi", [P, KD, TOK], F32R)
        with ExitStack() as s:
            y_ffn = sb("y_ffn", [P, NT, W], F32, s)
            zt_ffn = sb("zt_ffn", [P, D], F32, s)
        aT_lo = sb("aT_lo", [P, KD, TOK], F32R)

        with ExitStack() as s:
            qT = sb("qT", [P, HP, TOK], F32, s)
            with ExitStack() as s2:
                xc = sb("xc", [P, NT, W], F32, s2)
            with ExitStack() as s2:
                vn = sb("vn", [P, NT, W], F32, s2)
            kT = sb("kT", [P, HP, TOK], F32, s)
            vt = sb("vt", [P, NT, H, DH + 1], F32, s)
            sg = sb("sg", [P, NT, W], F32, s)
            with ExitStack() as s2:
                xsq = sb("xsq", [P, NT, W], F32, s2)
            with ExitStack() as s2:
                toe = sb("toe", [P, 2, DIST], F32, s2)
                qf = sb("qf", [P, 2, 2, LAT], F32, s2)
                pr = sb("pr", [P, 4, LAT], F32, s2)
                kp = sb("kp", [P, H, DH], F32, s2)
                kd = sb("kd", [P, 2, H, DH], F32, s2)
            with ExitStack() as s2:
                bias_raw = sb("bias_raw", [P, H * ROWS, 3 * CB], F32, s2)
                bias = sb("bias", [P, H, NBIAS, P], F32, s2)
                stt = sb("stt", [P, W], F32, s2)
                with ExitStack() as s3:
                    tm = sb("tm", [P, NT, W], F32, s3)
                sp = sb("sp", [P, 2, W], F32, s2)
                pt = sb("pt", [P, 2, W], F32, s2)
                on = sb("on", [P, 2, W], F32, s2)
                t1 = sb("t1", [P, 2, W], F32, s2)
        with ExitStack() as s:
            xn = sb("xn", [P, NT, D], F32, s)
            tf = sb("tf", [P, 2, TOK], F32, s)
            y_mix = sb("y_mix", [P, NT, W], F32, s)
            zt = sb("zt", [P, D], F32, s)
            gb_mix = sb("gb_mix", [P, 2, D], F32, s)
        with ExitStack() as s:
            m = sb("m", [P, KF, TOK], F32, s)
            cv = sb("cv", [P, 4, TOK], F32, s)
            gb_ffn = sb("gb_ffn", [P, 2, D], F32, s)

        bank = [ctx.enter_context(nc.psum_tensor(f"bank{i}", [P, 512], F32)) for i in range(8)]
        ADA_BANK = 7
        CTX_BANK = (4, 7)


        PER, PRIME = {}, {}

        def counted(name, per, prime=0):
            s_ = sem(name)
            PER[s_], PRIME[s_] = per, prime
            return s_

        const_in = sem("const_in")
        y_out = sem("y_out")
        cond_silu = sem("cond_silu")
        raw_full = [counted(f"raw_full{i}", 16 * ROUNDS) for i in range(SLOTS)]
        raw_free = [counted(f"raw_free{i}", ROUNDS, 1) for i in range(SLOTS)]
        hi_done = counted("hi_done", GW)
        w_used = counted("w_used", GW, 4)
        par_in = counted("par_in", 16 * 6)
        bias_in = counted("bias_in", 16)
        kv_out = counted("kv_out", 16 * 3)
        v_moved = counted("v_moved", 16 * (1 + ROWS * NQB))
        mod_done = counted("mod_done", 7)
        lg_step = counted("lg_step", 19)
        lg_exp = counted("lg_exp", 1)
        kdec_done = counted("kdec_done", 1)
        pre_sq = counted("pre_sq", 2 * NT)
        pre_std = counted("pre_std", 2 * NT)
        pre_rstd = counted("pre_rstd", 2 * NT)
        xn_done = counted("xn_done", 2 * NT)
        norm_tp = counted("norm_tp", 2 * KD)
        norm_mod = counted("norm_mod", 2 * KD)
        norm_hi = counted("norm_hi", 2 * KD)
        norm_lo = counted("norm_lo", 2 * KD)
        in_done = counted("in_done", NB_IN * (NT - 1))
        rope_part = counted("rope_part", 2 * 4 * 3)
        rope_done = counted("rope_done", 2 * NT)
        in_copied = counted("in_copied", 5 * NT)
        qk_tp = counted("qk_tp", 4 * NT)
        qk_T = counted("qk_T", 4 * NT)
        kp_done = counted("kp_done", 1)
        kd_done = counted("kd_done", 1)
        toe_lin = counted("toe_lin", H)
        toe_min = counted("toe_min", H)
        toe_exp = counted("toe_exp", H)
        toe_done = counted("toe_done", H)
        qf_exp = counted("qf_exp", HP)
        qf_done = counted("qf_done", HP)
        ret_s = counted("ret_s", 5 * H)
        ret_p = counted("ret_p", 5 * H)
        ret_av = counted("ret_av", 5 * H)
        st_mm = counted("st_mm", 1)
        st_done = counted("st_done", 1)
        gn_read = counted("gn_read", NT)
        gn_step = counted("gn_step", 5 * NT)
        gn_sq = counted("gn_sq", NT)
        gn_std = counted("gn_std", NT)
        ret_done = counted("ret_done", NT)
        ones_set = counted("ones_set", 2)
        bias_done = counted("bias_done", NBIAS)
        mix_tp = counted("mix_tp", 2 * NT)
        mix_hi = counted("mix_hi", 2 * NT)
        mix_lo = counted("mix_lo", 2 * NT)
        NU = len(UNITS)
        na_s = counted("na_s", NU)
        na_c = counted("na_c", NQB * H)
        na_m = counted("na_m", NU)
        na_e = counted("na_e", NU)
        na_t = counted("na_t", NU)
        na_p = counted("na_p", NU)
        na_av = counted("na_av", NU)
        na_r = counted("na_r", NU // 4)
        na_o = counted("na_o", NU // 4)
        gb_mm = counted("gb_mm", 8)
        gb_done = counted("gb_done", 8)
        y_done = counted("y_done", 4 * (NT - 1))
        y_sq = counted("y_sq", 4 * NT)
        y_copied = counted("y_copied", 2 * NT)
        y_base = counted("y_base", 2)
        post_std = counted("post_std", 2 * NT)
        post_rstd = counted("post_rstd", 2 * NT)
        post_y = counted("post_y", 4 * NT)
        x_done = counted("x_done", 2 * NT, 2 * NT)
        tap_mid = counted("tap_mid", G_UP)
        tap_left = counted("tap_left", 2 * G_UP)
        conv_done = counted("conv_done", G_UP, 4)
        silu_done = counted("silu_done", KF)
        m_done = counted("m_done", KF, 2)
        mhi_done = counted("mhi_done", 2 * KF)
        mlo_done = counted("mlo_done", 2 * KF)
        primed = sem("primed")

        block = ctx.enter_context(nc.Block())

        def stage(eng, layer):
            reg = eng.alloc_register()
            eng.reg_mov(reg, layer)
            return eng.snap(reg, min_val=0, max_val=DEPTH - 1)

        def at(s_, layer, n):
            return layer * PER[s_] + (n + PRIME[s_])

        def full(s, layer):
            return raw_full[s % SLOTS], at(raw_full[s % SLOTS], layer, 16 * (s // SLOTS + 1))

        def freed(s, layer):
            return raw_free[s % SLOTS], at(raw_free[s % SLOTS], layer, s // SLOTS + 1)

        def stream_of(g):
            if g < W_OUT0:
                return stream_in(g // 4, g % 4)
            return g + ADA

        def cols(s, n=1024):
            return (slice(None), s % SLOTS, slice(0, n))

        halves = [(DH * (h % 2), h // 2) for h in range(H)]

        def in_bank(b, tt):
            return (NT * b + tt) % 7

        def qk_bank(b, tt):
            return (NT * (b + 2) + tt % 2) % 7

        qk_blocks = [0, 1, 5, 6]
        GB_BANKS = [5, 6, 7, 4]
        out_bank = [[0, 1, 2, 3, 4], [5, 6, 7, 0, 1]]

        @block.sync
        def _(sp_):
            for dst, src in [(ident[:], t["ident"]), (rope[:], t["rope"]), (dist[:], t["dist"]), (qpos[:], t["qpos"]),
                             (kpos[:], t["kpos"]), (masks[:], t["masks"]), (cond[:], t["cond"]),
                             (x[:, 0, :], t["xp"]), (x[:, 1:NT, :], t["xs"].rearrange("(i p) d -> p i d", p=P))]:
                sp_.dma_start(dst, src).then_inc(const_in, 16)
            sp_.wait_ge(primed, 1)

            def stream(layer, first, last):
                with sp_.Fori(first, last) as r:
                    rnd = sp_.snap(layer * ROUNDS + r)
                    for s in range(SLOTS):
                        src = t["stream"][s, bass.ds(rnd, 1), :, :].rearrange("o p n -> p (o n)")
                        sp_.wait_ge(raw_free[s], rnd + 1)
                        sp_.dma_start(raw[:, s, :], src).then_inc(raw_full[s], 16)

            with sp_.Fori(0, DEPTH) as layer:
                lay = bass.ds(layer, 1)
                for dst, src in [(par[:], t["par"][lay].rearrange("o p n -> p (o n)")),
                                 (dec[:, 0, :], t["dec_f"][lay].to_broadcast([P, H])),
                                 (dec[:, 1, :], t["dec_b"][lay].to_broadcast([P, H])),
                                 (st0[:], t["st0"][lay].rearrange("o p n -> p (o n)")),
                                 (ctx_kT[:], t["ctx_kT"][lay].rearrange("o p n -> p (o n)")),
                                 (ctx_v[:, :, 0:DH], t["ctx_v"][lay].rearrange("o p h d -> (o p) h d"))]:
                    sp_.dma_start(dst, src).then_inc(par_in, 16)
                stream(layer, 0, 17)
                sp_.dma_start(bias_raw[:], t["bias"][lay].rearrange("o p n -> p (o n)")).then_inc(bias_in, 16)
                sp_.wait_ge(st_done, at(st_done, layer, 1))
                sp_.dma_start(t["st"][lay].rearrange("o p n -> (o p) n"), stt[:]).then_inc(kv_out, 16)
                sp_.wait_ge(in_copied, at(in_copied, layer, 3 * NT))
                sp_.dma_start(t["nv"][lay].rearrange("o p n -> (o p) n"), vn[:, 0, :]).then_inc(kv_out, 16)
                sp_.dma_start(vt[:, 0, :, 0:DH], vn[:, 0, :].rearrange("p (h d) -> p h d", h=H)).then_inc(v_moved, 16)
                for r in range(ROWS):
                    tt, p0 = 1 + r // 2, GRID_W * (r % 2)
                    for jb in range(NQB):
                        sp_.dma_start(vt[CB * r:CB * (r + 1), 1 + jb, :, 0:DH],
                                      vn[p0 + CB * jb:p0 + CB * (jb + 1), tt, :].rearrange("p (h d) -> p h d", h=H)
                                      ).then_inc(v_moved, 16)
                stream(layer, 17, 20)
                sp_.wait_ge(in_copied, at(in_copied, layer, 4 * NT + 1))
                sp_.dma_start(t["nk"][lay].rearrange("o p n -> (o p) n"), tm[:, 0, :]).then_inc(kv_out, 16)
                stream(layer, 20, ROUNDS)
            for tt in range(NT):
                sp_.wait_ge(x_done, DEPTH * 2 * NT + NT + tt + 1)
                dst = t["yp"] if tt == 0 else t["ys"][(tt - 1) * P:tt * P, :]
                sp_.dma_start(dst, x[:, tt, :]).then_inc(y_out, 16)
            sp_.wait_ge(y_out, 16 * NT)
            sp_.wait_ge(kv_out, 16 * 3 * DEPTH)

        @block.gpsimd
        def _(pool):
            for n, (s_, k) in enumerate((s_, k) for s_, k in PRIME.items() if k):
                pool.memset(prime[:, n:n + 1], 0.0).then_inc(s_, k)
            pool.memset(eps[:], EPS).then_inc(primed, 1)
            with pool.Fori(0, DEPTH) as layer:
                pool.wait_ge(par_in, at(par_in, layer, 96))
                pool.wait_ge(bias_in, at(bias_in, layer, 16))
                for e_, part in enumerate([1, 0, 1, 2, 1]):
                    pool.tensor_tensor(
                        bias[:, :, e_, :].rearrange("p h (r c) -> p h r c", c=CB),
                        bias_raw[:].rearrange("p (h r) k -> p h r k", h=H)[:, :, :, part * CB:(part + 1) * CB],
                        masks[:, e_, :].unsqueeze(1).unsqueeze(1).to_broadcast([P, H, ROWS, CB]),
                        ALU.add).then_inc(bias_done, 1)
                pool.memset(ctx_v[:, :, DH:DH + 1], 1.0).then_inc(ones_set, 1)
                pool.memset(vt[:, :, :, DH:DH + 1], 1.0).then_inc(ones_set, 1)

        MOD_PRE, MOD_MID, MOD_ALL = 2, 3, 7
        LG_ABS, LG_ALL = 2, 19

        def tile_done(b, tt, layer):
            if tt < NT - 1:
                return in_done, at(in_done, layer, (NT - 1) * b + tt + 1)
            return w_used, at(w_used, layer, 4 * b + 4)

        def half_done(w, n, tt, layer):
            if tt < NT - 1:
                return y_done, at(y_done, layer, (NT - 1) * (2 * w + n) + tt + 1)
            last = W_DOWN0 + len(DOWN_KT) * (n + 1) if w else W_OUT0 + 4 * (n + 1)
            return w_used, at(w_used, layer, last)

        def kt_free(q, layer):
            n, kt = divmod(q, KF)
            if n == 0 and kt < 4:
                return at(w_used, layer, W_DOWN0)
            if kt >= 4:
                kt -= 4
            else:
                n, kt = 0, max(k for k in range(KF) if k % 4 == kt)
            gi = next(i for i, kts in enumerate(DOWN_KT) if kt in kts)
            return at(w_used, layer, W_DOWN0 + len(DOWN_KT) * n + gi + 1)

        def x_ready(w, tt, layer):
            return at(x_done, layer, NT * w + tt + 1 - NT)

        def width(g):
            return 512 if g >= W_DOWN0 and (g - W_DOWN0) % len(DOWN_KT) >= 10 else 1024

        def blk(ap):
            return ap.rearrange("p (a q) -> p a q", a=4)

        def grid(ap, jb):
            return ap.rearrange("p (r c) -> p r c", c=GRID_W)[:, :, CB * jb:CB * (jb + 1)]

        def tap(i, c, j):
            return par[:, bass.ds(2 * j + (C_TAP + (i * 2 + c % 2) * KF + c // 2), 1)]

        @block.scalar
        def _(act):
            act.wait_ge(const_in, 16 * 9)
            act.wait_ge(primed, 1)
            act.activation(cond[:], cond[:], ACT.Silu).then_inc(cond_silu, 1)

            def split_hi(g, layer):
                s, n = stream_of(g), width(g)
                act.wait_ge(*full(s, layer))
                act.wait_ge(w_used, at(w_used, layer, g - 3))
                act.activation(w_hi[:, g % 4, 0:n], raw[:, s % 4, 0:n], ACT.Copy).then_inc(hi_done, 1)

            def pre_norm(w, layer):
                for tt in range(NT):
                    i = NT * w + tt
                    act.wait_ge(x_done, x_ready(w, tt, layer))
                    act.activation(sq[:], x[:, tt, :], ACT.Square, accum_out=ssq[:, 0, tt:tt + 1]).then_inc(pre_sq, 1)
                    act.wait_ge(pre_sq, at(pre_sq, layer, i + 1))
                    act.activation(std[:, tt:tt + 1], ssq[:, 0, tt:tt + 1], ACT.Sqrt, bias=eps[:],
                                   scale=1.0 / D).then_inc(pre_std, 1)
                first = W_UP0 if w else 0
                for g in range(first, first + 2):
                    split_hi(g, layer)
                for k in range(KD):
                    i = KD * w + k
                    act.wait_ge(norm_mod, at(norm_mod, layer, i + 1))
                    act.activation(aT_hi[:, k, :], tf[:, k % 2, :], ACT.Copy).then_inc(norm_hi, 1)
                for g in range(first + 2, first + 4):
                    split_hi(g, layer)

            def toe_table(h, layer):
                if h >= 2:
                    act.wait_ge(ret_p, at(ret_p, layer, 5 * (h - 1)))
                act.activation(toe[:, h % 2, :], dist[:], ACT.Copy, scale=lg[:, 0, h:h + 1]).then_inc(toe_lin, 1)
                act.wait_ge(toe_min, at(toe_min, layer, h + 1))
                act.activation(toe[:, h % 2, :], toe[:, h % 2, :], ACT.Exp).then_inc(toe_exp, 1)

            def query_decay(a, layer):
                if a >= 2:
                    act.wait_ge(ret_av, at(ret_av, layer, 10 * (a - 1)))
                act.activation(qf[:, a % 2, 0, :], qpos[:, 0, :], ACT.Exp, scale=lgp[:, 0, a:a + 1])
                act.activation(qf[:, a % 2, 1, :], qpos[:, 1, :], ACT.Exp,
                               scale=lgp[:, 1, a:a + 1]).then_inc(qf_exp, 1)

            def qk_evac(b, layer):
                dst = qT if b in (0, 5) else kT
                scale = SCALE if b in (0, 5) else 1.0
                if b == 6:
                    act.wait_ge(v_moved, at(v_moved, layer, PER[v_moved]))
                    act.wait_ge(kv_out, at(kv_out, layer, 32))
                for tt in range(NT):
                    act.wait_ge(qk_tp, at(qk_tp, layer, NT * qk_blocks.index(b) + tt + 1))
                    src = blk(bank[qk_bank(b, tt)][:])
                    if b < 2 or tt == 0:
                        act.activation(dst[:, :, tt * P:(tt + 1) * P], src, ACT.Copy, scale=scale).then_inc(qk_T, 1)
                        continue
                    for i in range(2):
                        i_ = act.activation(
                            dst[:, :, P:TOK].rearrange("p a (j r c) -> p a j r c", j=NQB, r=ROWS)[:, :, :, 2 * tt - 2 + i, :],
                            src.rearrange("p a (i j c) -> p a i j c", i=2, j=NQB)[:, :, i, :, :], ACT.Copy, scale=scale)
                    i_.then_inc(qk_T, 1)

            def gate_rows(w, layer):
                gb = gb_ffn if w else gb_mix
                for i in range(4):
                    act.wait_ge(gb_mm, at(gb_mm, layer, 4 * w + i + 1))
                    act.activation(gb[:, i // 2, (i % 2) * W:(i % 2 + 1) * W], bank[GB_BANKS[i]][:],
                                   ACT.Copy).then_inc(gb_done, 1)

            def half_squares(w, n, layer):
                for tt in range(NT):
                    b = tt if w else out_bank[n][tt]
                    i = 2 * NT * w + NT * n + tt
                    act.wait_ge(*half_done(w, n, tt, layer))
                    act.activation(sq[:, 0:W], bank[b][:], ACT.Square,
                                   accum_out=ssq[:, n, tt:tt + 1]).then_inc(y_sq, 1)
                    act.wait_ge(y_sq, at(y_sq, layer, i + 1))
                    if n == 1:
                        act.wait_ge(y_base, at(y_base, layer, w + 1))
                        act.activation(std[:, tt:tt + 1], ssq[:, 1, tt:tt + 1], ACT.Sqrt, bias=base[:, tt:tt + 1],
                                       scale=1.0 / D).then_inc(post_std, 1)

            with act.Fori(0, DEPTH) as the_layer:
                layer = stage(act, the_layer)
                pre_norm(0, layer)
                act.wait_ge(lg_step, at(lg_step, layer, LG_ABS))
                act.activation(lgt[:, 2, :], lgt[:, 1, :], ACT.Exp, scale=-1.0).then_inc(lg_exp, 1)
                for b in range(NB_IN):
                    layer = stage(act, the_layer)
                    if b - 1 in qk_blocks:
                        qk_evac(b - 1, layer)
                    for q in range(3):
                        split_hi(4 * (b + 1) + q, layer)
                    if b == 3:
                        act.wait_ge(lg_step, at(lg_step, layer, LG_ALL))
                        for d in range(2):
                            i_ = act.activation(kdec[:, d, :], lg[:, d, :], ACT.Exp, scale=kpos[:, d:d + 1])
                        i_.then_inc(kdec_done, 1)
                        toe_table(0, layer)
                        query_decay(0, layer)
                    for tt in range(NT):
                        if b < 2:
                            break
                        act.wait_ge(*tile_done(b, tt, layer))
                        src = bank[in_bank(b, tt)][:]
                        if b == 3:
                            act.activation(sg[:, tt, :], src, ACT.Silu).then_inc(in_copied, 1)
                            continue
                        if b == 2:
                            act.activation(vt[:, tt, :, 0:DH], src.rearrange("p (h d) -> p h d", h=H),
                                           ACT.Copy).then_inc(in_copied, 1)
                        else:
                            act.activation((vn if b == 4 else tm)[:, tt, :], src, ACT.Copy).then_inc(in_copied, 1)
                    split_hi(4 * (b + 1) + 3, layer)
                    if b == 3:
                        layer = stage(act, the_layer)
                        for h in range(H):
                            if h + 1 < H:
                                toe_table(h + 1, layer)
                            if h % 2 == 0 and h // 2 + 1 < HP:
                                query_decay(h // 2 + 1, layer)
                        for i in range(NT):
                            tt = (i + 1) % NT
                            act.wait_ge(gn_read, at(gn_read, layer, i + 1))
                            act.activation(xsq[:, tt, :], xc[:, tt, :], ACT.Square).then_inc(gn_sq, 1)
                        act.wait_ge(st_mm, at(st_mm, layer, 1))
                        act.activation(stt[:], bank[5][:], ACT.Copy).then_inc(st_done, 1)
                        for i in range(NT):
                            tt = (i + 1) % NT
                            act.wait_ge(gn_step, at(gn_step, layer, 2 * NT + i + 1))
                            act.activation(gn[:, 3, tt, :], gn[:, 2, tt, :], ACT.Sqrt, bias=eps[:],
                                           scale=1.0 / DH).then_inc(gn_std, 1)
                qk_evac(6, layer)
                layer = stage(act, the_layer)
                for tt in range(NT):
                    act.wait_ge(mix_tp, at(mix_tp, layer, tt + 1))
                    act.activation(aT_hi[:, 0:HP, tt * P:(tt + 1) * P], blk(bank[3 + tt % 2][:]),
                                   ACT.Copy).then_inc(mix_hi, 1)
                layer = stage(act, the_layer)
                for i in range(NU + 6):
                    if i < NU:
                        jb, h = UNITS[i]
                        n = P * len(key_blocks(jb)[0])
                        act.wait_ge(na_m, at(na_m, layer, i + 1))
                        e_ = act.activation(sp[:, i % 2, 0:P], bank[i % 3][:, 0:P], ACT.Exp, bias=nmax[:, i % 4:i % 4 + 1])
                        if n:
                            e_ = act.activation(sp[:, i % 2, P:P + n], sp[:, i % 2, P:P + n], ACT.Exp,
                                                bias=nmax[:, i % 4:i % 4 + 1], scale=-1.0)
                        e_.then_inc(na_e, 1)
                    if 1 <= i <= NU:
                        u = i - 1
                        n = P * (1 + len(key_blocks(UNITS[u][0])[0]))
                        act.wait_ge(na_t, at(na_t, layer, u + 1))
                        if u >= 2:
                            act.wait_ge(na_av, at(na_av, layer, u - 1))
                        act.activation(pt[:, u % 2, 0:n], bank[3 + u % 2][:, 0:n], ACT.Copy).then_inc(na_p, 1)
                    if i % 8 == 5 and i >= 8:
                        jb = i // 8 - 1
                        act.wait_ge(mix_tp, at(mix_tp, layer, NT + jb + 1))
                        src = blk(bank[7][:])
                        if jb == NQB:
                            act.activation(aT_hi[:, HP:KD, 0:P], src, ACT.Copy).then_inc(mix_hi, 1)
                        else:
                            for a in range(HP):
                                e_ = act.activation(grid(aT_hi[:, HP + a, P:TOK], jb),
                                                    src[:, a, :].rearrange("p (r c) -> p r c", c=CB), ACT.Copy)
                            e_.then_inc(mix_hi, 1)
                layer = stage(act, the_layer)
                gate_rows(0, layer)
                for g in range(W_OUT0 + 4, W_OUT0 + 7):
                    split_hi(g, layer)
                half_squares(0, 0, layer)
                split_hi(W_OUT0 + 7, layer)
                half_squares(0, 1, layer)
                layer = stage(act, the_layer)
                pre_norm(1, layer)
                with act.Fori(0, KF // 2) as j:
                    def gate_silu(c):
                        act.wait_ge(conv_done, at(conv_done, layer, 4 * j + c + 1))
                        act.activation(cv[:, c, :], cv[:, c, :], ACT.Silu).then_inc(silu_done, 1)

                    for c in range(4):
                        act.wait_ge(w_used, at(w_used, layer, 4 * j + W_UP0 + c + 1))
                        act.wait_ge(m_done, at(m_done, layer, 2 * j + c // 2 - 1))
                        bias_ = par[:, bass.ds(2 * j + (C_CB + (c % 2) * KF + c // 2), 1)]
                        act.activation(cv[:, c, 0:CTX], bank[4 + c][:, 0:CTX], ACT.Identity, bias=bias_, scale=tap(1, c, j))
                        act.activation(cv[:, c, CTX:TOK], bank[c][:], ACT.Identity, bias=bias_,
                                       scale=tap(1, c, j)).then_inc(tap_mid, 1)
                        act.wait_ge(raw_full[c], at(raw_full[c], layer, 16 * (j + (S_UP0 // 4 + 2))))
                        act.activation(w_hi[:, c, :], raw[:, c, :], ACT.Copy).then_inc(hi_done, 1)
                        if c == 2:
                            gate_silu(1)
                    gate_silu(3)
                gate_rows(1, layer)
                layer = stage(act, the_layer)
                for gi in range(G_DOWN):
                    if 2 <= gi and gi + 2 < G_DOWN:
                        split_hi(W_DOWN0 + gi + 2, layer)
                    n, i = divmod(gi, len(DOWN_KT))
                    for kt in DOWN_KT[i]:
                        q = KF * n + kt
                        act.wait_ge(w_used, kt_free(q, layer))
                        act.wait_ge(m_done, at(m_done, layer, kt + 1))
                        act.activation(m_hi[:, kt % 4, :], m[:, kt, :], ACT.Copy).then_inc(mhi_done, 1)
                    if gi == len(DOWN_KT):
                        half_squares(1, 0, layer)
                half_squares(1, 1, layer)

        @block.vector
        def _(dve):
            dve.wait_ge(const_in, 16 * 9)
            dve.wait_ge(primed, 1)

            def split_lo(g, layer):
                s, n = stream_of(g), width(g)
                dve.wait_ge(hi_done, at(hi_done, layer, g + 1))
                dve.tensor_tensor(w_lo[:, g % 4, 0:n], raw[:, s % 4, 0:n], w_hi[:, g % 4, 0:n].bitcast(F32),
                                  ALU.subtract).then_inc(raw_free[s % 4], 1)

            def add_ada_bias(lo, hi_):
                return dve.tensor_tensor(mod[:, lo:hi_, :],
                                         bank[ADA_BANK][:, 2 * lo:2 * hi_].rearrange("p (f c) -> p f c", c=2),
                                         par[:, C_AB + lo:C_AB + hi_].unsqueeze(2).to_broadcast([P, hi_ - lo, 2]), ALU.add)

            def times_gain(f0, c0, plus):
                return dve.scalar_tensor_tensor(mod[:, f0:f0 + KD, :], mod[:, f0:f0 + KD, :], plus,
                                                par[:, c0:c0 + KD].unsqueeze(2).to_broadcast([P, KD, 2]),
                                                ALU.add, ALU.mult)

            def pre_norm(w, layer):
                for tt in range(NT):
                    i = NT * w + tt
                    dve.wait_ge(pre_std, at(pre_std, layer, i + 1))
                    dve.reciprocal(rstd[:, tt:tt + 1], std[:, tt:tt + 1]).then_inc(pre_rstd, 1)
                    dve.wait_ge(pre_rstd, at(pre_rstd, layer, i + 1))
                    dve.tensor_scalar(xn[:, tt, :], x[:, tt, :], rstd[:, tt:tt + 1], None, ALU.mult).then_inc(xn_done, 1)
                if w == 0:
                    dve.wait_ge(*freed(ADA_FIRST - 1, layer))
                    add_ada_bias(0, ADA_FIRST).then_inc(mod_done, 1)
                    dve.wait_ge(mod_done, at(mod_done, layer, 1))
                    times_gain(KD, C_GM, 1.0).then_inc(mod_done, 1)
                    dve.wait_ge(mod_done, at(mod_done, layer, MOD_PRE))
                else:
                    dve.wait_ge(mod_done, at(mod_done, layer, MOD_ALL))
                sh = 3 * KD * w
                first = W_UP0 if w else 0
                for g in range(first, first + 2):
                    split_lo(g, layer)
                for k in range(KD + 1):
                    i = KD * w + k
                    if k < KD:
                        dve.wait_ge(norm_tp, at(norm_tp, layer, i + 1))
                        if k >= 2:
                            dve.wait_ge(norm_lo, at(norm_lo, layer, i - 1))
                        dve.tensor_scalar(tf[:, k % 2, 0:CTX], bank[CTX_BANK[k % 2]][:, 0:P],
                                          mod[:, sh + KD + k, 0:1], mod[:, sh + k, 0:1], ALU.mult, ALU.add)
                        dve.tensor_scalar(tf[:, k % 2, CTX:TOK], bank[5 + k % 2][:],
                                          mod[:, sh + KD + k, 1:2], mod[:, sh + k, 1:2], ALU.mult,
                                          ALU.add).then_inc(norm_mod, 1)
                    if k >= 1:
                        dve.wait_ge(norm_hi, at(norm_hi, layer, i))
                        dve.tensor_tensor(aT_lo[:, k - 1, :], tf[:, (k - 1) % 2, :], aT_hi[:, k - 1, :].bitcast(F32),
                                          ALU.subtract).then_inc(norm_lo, 1)
                for g in range(first + 2, first + 4):
                    split_lo(g, layer)

            def decays(layer):
                n = LG_ABS
                lg_in = dec[:].rearrange("p a h -> p (a h)")
                T = [lgt[:, i, :] for i in range(4)]

                def after():
                    dve.wait_ge(lg_step, at(lg_step, layer, n))
                dve.wait_ge(lg_exp, at(lg_exp, layer, 1))
                dve.tensor_scalar(T[0], T[2], 2.0, None, ALU.add).then_inc(lg_step, 1)
                n += 1
                after()
                dve.reciprocal(T[0], T[0]).then_inc(lg_step, 1)
                n += 1
                after()
                dve.tensor_tensor(T[1], T[2], T[0], ALU.mult).then_inc(lg_step, 1)
                n += 1
                after()
                dve.tensor_tensor(T[0], T[1], T[1], ALU.mult).then_inc(lg_step, 1)
                n += 1
                after()
                dve.tensor_scalar(T[3], T[0], 1.0 / 15, None, ALU.mult).then_inc(lg_step, 1)
                n += 1
                for c in (13, 11, 9, 7, 5, 3):
                    after()
                    dve.scalar_tensor_tensor(T[3], T[3], 1.0 / c, T[0], ALU.add, ALU.mult).then_inc(lg_step, 1)
                    n += 1
                after()
                dve.scalar_tensor_tensor(T[3], T[3], 1.0, T[1], ALU.add, ALU.mult).then_inc(lg_step, 1)
                n += 1
                dve.tensor_scalar(T[2], lg_in, 0.0, None, ALU.min).then_inc(lg_step, 1)
                n += 1
                after()
                dve.scalar_tensor_tensor(lg[:].rearrange("p a h -> p (a h)"), T[3], -2.0, T[2], ALU.mult,
                                         ALU.add).then_inc(lg_step, 1)
                n += 1
                after()
                dve.tensor_scalar(nlg[:], lg[:, 1, :], -1.0, None, ALU.mult).then_inc(lg_step, 1)
                for p in range(2):
                    dve.tensor_copy(lgp[DH * p:DH * (p + 1), :, :],
                                    lg[DH * p:DH * (p + 1), :, :].rearrange("p a (i e) -> p a i e", e=2)[:, :, :, p]
                                    ).then_inc(lg_step, 1)

            def rotate(b, layer):
                for tt in range(NT):
                    ps_ = bank[in_bank(b, tt)]
                    dve.wait_ge(*tile_done(b, tt, layer))
                    if b == 1:
                        dve.wait_ge(qk_tp, at(qk_tp, layer, tt + 1))
                    if tt == 0:
                        if b == 1:
                            dve.tensor_copy(kp[:], ps_[:].rearrange("p (h d) -> p h d", h=H)).then_inc(kp_done, 1)
                        dve.tensor_copy(tm[:, 0, :], ps_[:]).then_inc(rope_done, 1)
                        continue
                    n = 3 * (4 * b + tt - 1)
                    src = ps_[:].rearrange("p (h g e f) -> p h g e f", h=H, g=2, e=2)
                    swp = t1[:, 1, :].rearrange("p (h g e f) -> p h g e f", h=H, g=2, e=2)
                    sin = rope[:, 1, tt - 1, :].rearrange("p (g e f) -> p g e f", g=2, e=2)
                    if tt > 1:
                        dve.wait_ge(rope_done, at(rope_done, layer, NT * b + tt))
                    dve.tensor_tensor(t1[:, 0, :].rearrange("p (h d) -> p h d", h=H),
                                      ps_[:].rearrange("p (h d) -> p h d", h=H),
                                      rope[:, 0, tt - 1, :].unsqueeze(1).to_broadcast([P, H, DH]),
                                      ALU.mult).then_inc(rope_part, 1)
                    for e_ in range(2):
                        dve.tensor_tensor(swp[:, :, :, e_, :], src[:, :, :, 1 - e_, :],
                                          sin[:, :, e_, :].unsqueeze(1).to_broadcast([P, H, 2, 16]),
                                          ALU.mult).then_inc(rope_part, 1)
                    dve.wait_ge(rope_part, at(rope_part, layer, n + 3))
                    dve.tensor_tensor(tm[:, tt, :], t1[:, 0, :], t1[:, 1, :], ALU.add).then_inc(rope_done, 1)

            def toe_lower(h, layer):
                dve.wait_ge(toe_lin, at(toe_lin, layer, h + 1))
                dve.scalar_tensor_tensor(toe[:, h % 2, :], dist[:], nlg[:, h:h + 1], toe[:, h % 2, :],
                                         ALU.mult, ALU.min).then_inc(toe_min, 1)

            def toe_diagonal(h, layer):
                dve.wait_ge(toe_exp, at(toe_exp, layer, h + 1))
                dve.tensor_tensor(toe[:, h % 2, 3 * P:4 * P], toe[:, h % 2, 3 * P:4 * P], ident[:],
                                  ALU.add).then_inc(toe_done, 1)

            def decay_queries(a, layer):
                dve.wait_ge(qf_exp, at(qf_exp, layer, a + 1))
                dve.tensor_tensor(qf[:, a % 2, :, :], qf[:, a % 2, :, :],
                                  qT[:, a, P:TOK].unsqueeze(1).to_broadcast([P, 2, LAT]), ALU.mult).then_inc(qf_done, 1)

            def retention(layer):
                dve.wait_ge(kdec_done, at(kdec_done, layer, 1))
                for d in range(2):
                    i_ = dve.tensor_tensor(kd[:, d, :, :], kp[:], kdec[:, d, :].unsqueeze(2).to_broadcast([P, H, DH]),
                                           ALU.mult)
                i_.then_inc(kd_done, 1)
                for h in range(H):
                    if h + 1 < H:
                        toe_lower(h + 1, layer)
                    if h == 0:
                        dve.wait_ge(toe_done, at(toe_done, layer, 1))
                    for j in range(5):
                        u = 5 * h + j
                        n = LAT if j < 4 else P
                        off = 3 * P - P * j if j < 4 else 3 * P
                        dve.wait_ge(ret_s, at(ret_s, layer, u + 1))
                        if u >= 4:
                            dve.wait_ge(ret_av, at(ret_av, layer, u - 3))
                        if j == 0 and h:
                            dve.wait_ge(toe_done, at(toe_done, layer, h + 1))
                        dve.tensor_tensor(pr[:, u % 4, 0:n], bank[5 + u % 3][:, 0:n], toe[:, h % 2, off:off + n],
                                          ALU.mult).then_inc(ret_p, 1)
                    if h + 1 < H:
                        toe_diagonal(h + 1, layer)
                    if h % 2 == 0 and h // 2 + 1 < HP:
                        decay_queries(h // 2 + 1, layer)

            def group_norm(layer):
                dve.wait_ge(ret_av, at(ret_av, layer, 5 * H))
                for i in range(NT):
                    tt = (i + 1) % NT
                    o = bank[(tt - 1) % NT][:].rearrange("p (h d) -> p h d", h=H)
                    dve.tensor_reduce(gn[:, 0, tt, :], o, AX.X, ALU.add).then_inc(gn_step, 1)
                    dve.wait_ge(gn_step, at(gn_step, layer, 2 * i + 1))
                    dve.tensor_scalar(gn[:, 1, tt, :], gn[:, 0, tt, :], -1.0 / DH, None, ALU.mult).then_inc(gn_step, 1)
                    dve.wait_ge(gn_step, at(gn_step, layer, 2 * i + 2))
                    dve.tensor_tensor(xc[:, tt, :].rearrange("p (h d) -> p h d", h=H), o,
                                      gn[:, 1, tt, :].unsqueeze(2).to_broadcast([P, H, DH]),
                                      ALU.add).then_inc(gn_read, 1)
                for i in range(NT):
                    tt = (i + 1) % NT
                    dve.wait_ge(gn_sq, at(gn_sq, layer, i + 1))
                    dve.tensor_reduce(gn[:, 2, tt, :], xsq[:, tt, :].rearrange("p (h d) -> p h d", h=H), AX.X,
                                      ALU.add).then_inc(gn_step, 1)
                for i in range(NT):
                    tt = (i + 1) % NT
                    n = 3 * NT + 2 * i
                    dve.wait_ge(gn_std, at(gn_std, layer, i + 1))
                    dve.reciprocal(gn[:, 3, tt, :], gn[:, 3, tt, :]).then_inc(gn_step, 1)
                    dve.wait_ge(gn_step, at(gn_step, layer, n + 1))
                    x3 = xc[:, tt, :].rearrange("p (h d) -> p h d", h=H)
                    dve.tensor_tensor(x3, x3, gn[:, 3, tt, :].unsqueeze(2).to_broadcast([P, H, DH]),
                                      ALU.mult).then_inc(gn_step, 1)
                    dve.wait_ge(gn_step, at(gn_step, layer, n + 2))
                    dve.tensor_tensor(sg[:, tt, :], xc[:, tt, :], sg[:, tt, :], ALU.mult).then_inc(ret_done, 1)

            def post_norm(w, layer):
                gb, y, z = (gb_ffn, y_ffn, zt_ffn) if w else (gb_mix, y_mix, zt)
                dve.wait_ge(gb_done, at(gb_done, layer, 4 * w + 4))
                for tt in range(NT):
                    c, i = (0 if tt == 0 else 1), NT * w + tt
                    dve.wait_ge(post_std, at(post_std, layer, i + 1))
                    dve.reciprocal(rstd[:, tt:tt + 1], std[:, tt:tt + 1]).then_inc(post_rstd, 1)
                    dve.wait_ge(post_rstd, at(post_rstd, layer, i + 1))
                    if tt:
                        dve.wait_ge(x_done, at(x_done, layer, i))
                    src = bank[tt if w else out_bank[1][tt]][:]
                    dve.scalar_tensor_tensor(z[:, 0:W], y[:, tt, :], rstd[:, tt:tt + 1], gb[:, c, 0:W],
                                             ALU.mult, ALU.mult).then_inc(post_y, 1)
                    dve.scalar_tensor_tensor(z[:, W:D], src, rstd[:, tt:tt + 1], gb[:, c, W:D],
                                             ALU.mult, ALU.mult).then_inc(post_y, 1)
                    dve.wait_ge(post_y, at(post_y, layer, 2 * i + 2))
                    dve.tensor_tensor(x[:, tt, :], x[:, tt, :], z[:], ALU.add).then_inc(x_done, 1)

            def first_half(w, layer):
                y = y_ffn if w else y_mix
                for tt in range(NT):
                    dve.wait_ge(y_sq, at(y_sq, layer, 2 * NT * w + tt + 1))
                    dve.tensor_copy(y[:, tt, :], bank[tt][:]).then_inc(y_copied, 1)
                dve.wait_ge(y_sq, at(y_sq, layer, 2 * NT * w + NT))
                dve.tensor_scalar(base[:], ssq[:, 0, :], 1.0 / D, EPS, ALU.mult, ALU.add).then_inc(y_base, 1)

            with dve.Fori(0, DEPTH) as the_layer:
                layer = stage(dve, the_layer)
                dve.wait_ge(par_in, at(par_in, layer, 96))
                lg_in = dec[:].rearrange("p a h -> p (a h)")
                dve.tensor_scalar(lgt[:, 0, :], lg_in, -1.0, None, ALU.mult).then_inc(lg_step, 1)
                dve.wait_ge(lg_step, at(lg_step, layer, 1))
                dve.tensor_tensor(lgt[:, 1, :], lg_in, lgt[:, 0, :], ALU.max).then_inc(lg_step, 1)
                pre_norm(0, layer)
                for b in range(NB_IN):
                    layer = stage(dve, the_layer)
                    for q in range(3):
                        split_lo(4 * (b + 1) + q, layer)
                    if b < 2:
                        rotate(b, layer)
                    if b == 2:
                        decays(layer)
                    if b == 3:
                        toe_lower(0, layer)
                        toe_diagonal(0, layer)
                        decay_queries(0, layer)
                    split_lo(4 * (b + 1) + 3, layer)
                    if b == 3:
                        dve.wait_ge(*freed(stream_ada(3, 3), layer))
                        add_ada_bias(20, 36).then_inc(mod_done, 1)
                        retention(stage(dve, the_layer))
                        group_norm(stage(dve, the_layer))
                dve.wait_ge(*freed(stream_ada(6, 3), layer))
                add_ada_bias(36, ADA).then_inc(mod_done, 1)
                dve.wait_ge(mod_done, at(mod_done, layer, 4))
                times_gain(4 * KD, C_GF, 1.0).then_inc(mod_done, 1)
                times_gain(2 * KD, C_PM, 0.0).then_inc(mod_done, 1)
                times_gain(5 * KD, C_PF, 0.0).then_inc(mod_done, 1)
                layer = stage(dve, the_layer)
                for tt in range(NT):
                    dve.wait_ge(mix_hi, at(mix_hi, layer, tt + 1))
                    dst = (slice(None), slice(0, HP), slice(tt * P, (tt + 1) * P))
                    dve.tensor_tensor(aT_lo[dst], blk(bank[3 + tt % 2][:]), aT_hi[dst].bitcast(F32),
                                      ALU.subtract).then_inc(mix_lo, 1)
                layer = stage(dve, the_layer)
                dve.wait_ge(bias_done, at(bias_done, layer, NBIAS))
                dve.wait_ge(kv_out, at(kv_out, layer, 48))
                for i in range(NU + 6):
                    if i < NU:
                        jb, h = UNITS[i]
                        keys, e0 = key_blocks(jb)
                        n = P * len(keys)
                        dve.wait_ge(na_s, at(na_s, layer, i + 1))
                        if i >= 2:
                            dve.wait_ge(na_t, at(na_t, layer, i - 1))
                        if not keys:
                            dve.tensor_reduce(nmax[:, i % 4:i % 4 + 1], bank[i % 3][:, 0:P], AX.X, ALU.max,
                                              negate=True).then_inc(na_m, 1)
                        else:
                            dve.tensor_reduce(cmax[:, i % 4, 0:1], bank[i % 3][:, 0:P], AX.X, ALU.max, negate=True)
                            dve.tensor_tensor_reduce(sp[:, i % 2, P:P + n], bank[i % 3][:, P:P + n],
                                                     bias[:, h, e0:e0 + len(keys), :].rearrange("p e k -> p (e k)"),
                                                     -1.0, BIG, ALU.add, ALU.min, cmax[:, i % 4, 1:2]).then_inc(na_c, 1)
                            dve.wait_ge(na_c, at(na_c, layer, i + 1))
                            dve.tensor_tensor(nmax[:, i % 4:i % 4 + 1], cmax[:, i % 4, 0:1], cmax[:, i % 4, 1:2],
                                              ALU.min).then_inc(na_m, 1)
                    if i >= 6 and i % 4 == 2:
                        gi = i // 4 - 1
                        jb, half = gi // 2, gi % 2
                        dve.wait_ge(na_av, at(na_av, layer, 4 * gi + 4))
                        o = bank[5 + half][:, 0:4 * (DH + 1)].rearrange("p (h d) -> p h d", h=4)
                        dve.reciprocal(rec[:, half, :], o[:, :, DH]).then_inc(na_r, 1)
                        if gi >= 4 and half == 0:
                            dve.wait_ge(mix_tp, at(mix_tp, layer, NT + jb - 1))
                        dve.wait_ge(na_r, at(na_r, layer, gi + 1))
                        dve.tensor_tensor(on[:, jb % 2, 256 * half:256 * (half + 1)].rearrange("p (h d) -> p h d", h=4),
                                          o[:, :, 0:DH], rec[:, half, :].unsqueeze(2).to_broadcast([P, 4, DH]),
                                          ALU.mult).then_inc(na_o, 1)
                    if i % 8 == 5 and i >= 8:
                        jb = i // 8 - 1
                        dve.wait_ge(mix_hi, at(mix_hi, layer, NT + jb + 1))
                        src = blk(bank[7][:])
                        if jb == NQB:
                            dve.tensor_tensor(aT_lo[:, HP:KD, 0:P], src, aT_hi[:, HP:KD, 0:P].bitcast(F32),
                                              ALU.subtract).then_inc(mix_lo, 1)
                        else:
                            for a in range(HP):
                                i_ = dve.tensor_tensor(grid(aT_lo[:, HP + a, P:TOK], jb),
                                                       src[:, a, :].rearrange("p (r c) -> p r c", c=CB),
                                                       grid(aT_hi[:, HP + a, P:TOK].bitcast(F32), jb), ALU.subtract)
                            i_.then_inc(mix_lo, 1)
                layer = stage(dve, the_layer)
                for g in range(W_OUT0 + 4, W_OUT0 + 7):
                    split_lo(g, layer)
                first_half(0, layer)
                split_lo(W_OUT0 + 7, layer)
                post_norm(0, layer)
                layer = stage(dve, the_layer)
                pre_norm(1, layer)
                with dve.Fori(0, KF // 2) as j:
                    for c in range(4):
                        t_ = cv[:, c, :]
                        dve.wait_ge(tap_mid, at(tap_mid, layer, 4 * j + c + 1))
                        for lo, ps_ in ((0, bank[4 + c]), (CTX, bank[c])):
                            n = CTX if lo == 0 else LAT
                            dve.scalar_tensor_tensor(t_[:, lo + 1:lo + n], ps_[:, 0:n - 1], tap(0, c, j), t_[:, lo + 1:lo + n],
                                                     ALU.mult, ALU.add).then_inc(tap_left, 1)
                        for s, (lo, ps_) in enumerate(((0, bank[4 + c]), (CTX, bank[c]))):
                            n = CTX if lo == 0 else LAT
                            dve.wait_ge(tap_left, at(tap_left, layer, 8 * j + 2 * c + 1 + s))
                            i_ = dve.scalar_tensor_tensor(t_[:, lo:lo + n - 1], ps_[:, 1:n], tap(2, c, j), t_[:, lo:lo + n - 1],
                                                          ALU.mult, ALU.add)
                        i_.then_inc(conv_done, 1)
                        dve.wait_ge(hi_done, at(hi_done, layer, 4 * j + (W_UP0 + 4 + c + 1)))
                        dve.tensor_tensor(w_lo[:, c, :], raw[:, c, :], w_hi[:, c, :].bitcast(F32),
                                          ALU.subtract).then_inc(raw_free[c], 1)
                        if c >= 2:
                            s = c - 2
                            dve.wait_ge(silu_done, at(silu_done, layer, 2 * j + s + 1))
                            dve.tensor_tensor(m[:, bass.ds(2 * j + s, 1), :], cv[:, 2 * s:2 * s + 1, :],
                                              cv[:, 2 * s + 1:2 * s + 2, :], ALU.mult).then_inc(m_done, 1)
                layer = stage(dve, the_layer)
                for gi in range(G_DOWN):
                    if 2 <= gi and gi + 2 < G_DOWN:
                        split_lo(W_DOWN0 + gi + 2, layer)
                    n, i = divmod(gi, len(DOWN_KT))
                    for kt in DOWN_KT[i]:
                        q = KF * n + kt
                        dve.wait_ge(mhi_done, at(mhi_done, layer, q + 1))
                        dve.tensor_tensor(m_lo[:, kt % 4, :], m[:, kt, :], m_hi[:, kt % 4, :].bitcast(F32),
                                          ALU.subtract).then_inc(mlo_done, 1)
                    if gi == len(DOWN_KT):
                        first_half(1, layer)
                post_norm(1, layer)

        @block.tensor
        def _(pe):
            pe.wait_ge(const_in, 16 * 9)
            pe.wait_ge(cond_silu, 1)

            def mm3(out, lh, ll, rh, rl, start, stop):
                pe.matmul(out, ll, rh, start=start, stop=False)
                pe.matmul(out, lh, rl, start=False, stop=False)
                return pe.matmul(out, lh, rh, start=False, stop=stop)

            def ada(col, out, s):
                for k in range(KD):
                    i_ = pe.matmul(out, raw[:, s, k * P:(k + 1) * P], cond[:, :, k], start=k == 0, stop=k == KD - 1)
                i_.then_inc(raw_free[s], 1)

            def pre_norm_tp(w, layer):
                for k in range(KD):
                    i = KD * w + k
                    if k == 0:
                        pe.wait_ge(xn_done, at(xn_done, layer, NT * w + NT))
                    if k >= 2:
                        pe.wait_ge(norm_mod, at(norm_mod, layer, i - 1))
                    if k == 1 and w == 0:
                        pe.wait_ge(mod_done, at(mod_done, layer, 1))
                    ks = slice(k * P, (k + 1) * P)
                    pe.transpose(bank[CTX_BANK[k % 2]][:, 0:P], xn[:, 0, ks], ident[:])
                    for tt in range(1, NT):
                        i_ = pe.transpose(bank[5 + k % 2][:, (tt - 1) * P:tt * P], xn[:, tt, ks], ident[:])
                    i_.then_inc(norm_tp, 1)

            def qk_transposes(b, tts, layer):
                if tts[0] == 0:
                    if b < 2:
                        pe.wait_ge(rope_done, at(rope_done, layer, NT * (b + 1)))
                    else:
                        pe.wait_ge(in_copied, at(in_copied, layer, NT * (b - 1)))
                for tt in tts:
                    n = NT * qk_blocks.index(b) + tt
                    if tt >= 2:
                        pe.wait_ge(qk_T, at(qk_T, layer, n - 1))
                    out = bank[qk_bank(b, tt)]
                    for a in range(HP):
                        i_ = pe.transpose(out[:, a * P:(a + 1) * P], tm[:, tt, a * P:(a + 1) * P], ident[:])
                    i_.then_inc(qk_tp, 1)

            def bank_free(b, tt, layer):
                if b == 0:
                    if tt == 4:
                        pe.wait_ge(norm_mod, at(norm_mod, layer, KD))
                    return
                if b == 4:
                    if tt == 0:
                        pe.wait_ge(ret_p, at(ret_p, layer, 5 * H))
                    else:
                        pe.wait_ge(gn_read, at(gn_read, layer, tt))
                    return
                if b == 5 and tt < 2:
                    if tt == 0:
                        pe.wait_ge(gn_read, at(gn_read, layer, NT))
                    else:
                        pe.wait_ge(st_done, at(st_done, layer, 1))
                    return
                if tt < 2 and b - 2 in qk_blocks:
                    pe.wait_ge(qk_T, at(qk_T, layer, NT * qk_blocks.index(b - 2) + NT))
                n = NT * b + tt - 7
                if b == 1 and tt < 2:
                    pe.wait_ge(norm_mod, at(norm_mod, layer, KD))
                elif n < 2 * NT:
                    pe.wait_ge(rope_done, at(rope_done, layer, n + 1))
                else:
                    pe.wait_ge(in_copied, at(in_copied, layer, n - 2 * NT + 1))

            def in_granule(b, q, layer):
                g = 4 * b + q
                pe.wait_ge(*freed(stream_of(g), layer))
                for tt in range(NT):
                    if q == 0:
                        bank_free(b, tt, layer)
                    out, tok = bank[in_bank(b, tt)], slice(tt * P, (tt + 1) * P)
                    for kk in range(2):
                        k = 2 * q + kk
                        if b == 0 and tt == 0:
                            pe.wait_ge(norm_lo, at(norm_lo, layer, k + 1))
                        i_ = mm3(out[:], aT_hi[:, k, tok], aT_lo[:, k, tok],
                                 w_hi[:, g % 4, kk * W:(kk + 1) * W], w_lo[:, g % 4, kk * W:(kk + 1) * W],
                                 k == 0, k == KD - 1)
                    if tt == NT - 1:
                        i_.then_inc(w_used, 1)
                    elif q == 3:
                        i_.then_inc(in_done, 1)

            def in_ada(b, q, layer):
                s, col = stream_ada(b, q), ADA_FIRST + 4 * b + q
                pe.wait_ge(*full(s, layer))
                ada(col, bank[ADA_BANK][:, 2 * col:2 * col + 2], s % 4)

            def ret_scores(u, layer):
                h, j = divmod(u, 5)
                hs, a = halves[h]
                part = slice(hs, hs + DH)
                if u >= 3:
                    pe.wait_ge(ret_p, at(ret_p, layer, u - 2))
                if j < 4:
                    i_ = pe.matmul(bank[5 + u % 3][:], kT[part, a, P + P * j:2 * P + P * j], qT[part, a, P:TOK],
                                   start=True, stop=True)
                else:
                    i_ = pe.matmul(bank[5 + u % 3][:, 0:P], kT[part, a, 0:P], qT[part, a, 0:P], start=True, stop=True)
                i_.then_inc(ret_s, 1)

            def ret_values(u, layer):
                h, j = divmod(u, 5)
                hs, a = halves[h]
                part = slice(hs, hs + DH)
                col = slice(h * DH, (h + 1) * DH)
                pe.wait_ge(ret_p, at(ret_p, layer, u + 1))
                if j == 4:
                    pe.matmul(bank[4][:, col], pr[:, u % 4, 0:P], vt[:, 0, h, 0:DH], start=True,
                              stop=True).then_inc(ret_av, 1)
                    return
                if j == 0:
                    pe.wait_ge(qf_done, at(qf_done, layer, a + 1))
                    for i in range(4):
                        for d in range(2):
                            pe.matmul(bank[i][:, col], qf[part, a % 2, d, i * P:(i + 1) * P], st0[part, d, a, :],
                                      start=d == 0, stop=False, skip_group_check=True)
                for i in range(4):
                    i_ = pe.matmul(bank[i][:, col], pr[:, u % 4, i * P:(i + 1) * P], vt[:, 1 + j, h, 0:DH],
                                   start=False, stop=j == 3, skip_group_check=True)
                i_.then_inc(ret_av, 1)

            def retention(layer):
                pe.wait_ge(par_in, at(par_in, layer, 96))
                pe.wait_ge(in_copied, at(in_copied, layer, 2 * NT))
                pe.wait_ge(mod_done, at(mod_done, layer, MOD_MID))
                for u in range(5 * H + 2):
                    if u < 5 * H:
                        ret_scores(u, layer)
                    if u >= 2:
                        ret_values(u - 2, layer)
                pe.wait_ge(kd_done, at(kd_done, layer, 1))
                pe.wait_ge(ret_p, at(ret_p, layer, 5 * H))
                for d in range(2):
                    for h in range(H):
                        i_ = pe.matmul(bank[5][DH * d:DH * (d + 1), h * DH:(h + 1) * DH], kd[:, d, h, :],
                                       vt[:, 0, h, 0:DH], start=True, stop=True)
                i_.then_inc(st_mm, 1)

            def na_scores(u, layer):
                jb, h = UNITS[u]
                hs, a = halves[h]
                part = slice(hs, hs + DH)
                keys, _ = key_blocks(jb)
                if u >= 3:
                    pe.wait_ge(na_e, at(na_e, layer, u - 2))
                out = bank[u % 3]
                if jb == NQB:
                    pe.matmul(out[:, 0:P], qT[part, a, 0:P], kT[part, a, 0:P], start=True, stop=True).then_inc(na_s, 1)
                    return
                q_ = qT[part, a, P + P * jb:2 * P + P * jb]
                pe.matmul(out[:, 0:P], q_, ctx_kT[part, a, :], start=True, stop=True)
                if len(keys) == 3:
                    i_ = pe.matmul(out[:, P:4 * P], q_, kT[part, a, P * jb:P * (jb + 3)], start=True, stop=True)
                else:
                    for n, kb in enumerate(keys):
                        i_ = pe.matmul(out[:, P * (n + 1):P * (n + 2)], q_, kT[part, a, P + P * kb:2 * P + P * kb],
                                       start=True, stop=True)
                i_.then_inc(na_s, 1)

            def na_transposes(u, layer):
                n = 1 + len(key_blocks(UNITS[u][0])[0])
                pe.wait_ge(na_e, at(na_e, layer, u + 1))
                if u >= 2:
                    pe.wait_ge(na_p, at(na_p, layer, u - 1))
                for i in range(n):
                    i_ = pe.transpose(bank[3 + u % 2][:, i * P:(i + 1) * P], sp[:, u % 2, i * P:(i + 1) * P], ident[:])
                i_.then_inc(na_t, 1)

            def na_values(u, layer):
                jb, h = UNITS[u]
                keys, _ = key_blocks(jb)
                gi = u // 4
                pe.wait_ge(na_p, at(na_p, layer, u + 1))
                if u % 4 == 0 and gi >= 2:
                    pe.wait_ge(na_o, at(na_o, layer, gi - 1))
                out = bank[5 + gi % 2][:, (DH + 1) * (h % 4):(DH + 1) * (h % 4 + 1)]
                own = vt[:, 0, h, :] if jb == NQB else ctx_v[:, h, :]
                i_ = pe.matmul(out, pt[:, u % 2, 0:P], own, start=True, stop=not keys)
                for n, kb in enumerate(keys):
                    i_ = pe.matmul(out, pt[:, u % 2, P * (n + 1):P * (n + 2)], vt[:, 1 + kb, h, :],
                                   start=False, stop=n == len(keys) - 1)
                i_.then_inc(na_av, 1)

            def gate_rows(w, layer):
                for i in range(4):
                    c, n = i // 2, i % 2
                    for f in range(4):
                        v_ = mod[:, (5 if w else 2) * KD + 4 * n + f, c:c + 1].to_broadcast([P, P])
                        i_ = pe.matmul(bank[GB_BANKS[i]][:, f * P:(f + 1) * P], v_, ident[:], start=True, stop=True)
                    i_.then_inc(gb_mm, 1)

            with pe.Fori(0, DEPTH) as the_layer:
                layer = stage(pe, the_layer)
                with pe.Fori(0, ADA_FIRST // 4) as j:
                    for s in range(4):
                        pe.wait_ge(raw_full[s], at(raw_full[s], layer, 16 * (j + 1)))
                        ada(None, bank[ADA_BANK][:, bass.ds(8 * j + 2 * s, 2)], s)
                pre_norm_tp(0, layer)
                for b in range(NB_IN):
                    layer = stage(pe, the_layer)
                    in_granule(b, 0, layer)
                    post = b - 1 in qk_blocks
                    if post:
                        qk_transposes(b - 1, (0, 1), layer)
                    in_granule(b, 1, layer)
                    in_ada(b, 0, layer)
                    in_ada(b, 1, layer)
                    if post:
                        qk_transposes(b - 1, (2, 3), layer)
                    in_granule(b, 2, layer)
                    if post:
                        qk_transposes(b - 1, (4,), layer)
                    in_granule(b, 3, layer)
                    in_ada(b, 2, layer)
                    in_ada(b, 3, layer)
                    if b == 3:
                        retention(stage(pe, the_layer))
                qk_transposes(6, range(NT), layer)
                layer = stage(pe, the_layer)
                for tt in range(NT):
                    pe.wait_ge(ret_done, at(ret_done, layer, NT))
                    if tt >= 2:
                        pe.wait_ge(mix_lo, at(mix_lo, layer, tt - 1))
                    for a in range(HP):
                        i_ = pe.transpose(bank[3 + tt % 2][:, a * P:(a + 1) * P], sg[:, tt, a * P:(a + 1) * P], ident[:])
                    i_.then_inc(mix_tp, 1)
                layer = stage(pe, the_layer)
                pe.wait_ge(qk_T, at(qk_T, layer, 4 * NT))
                pe.wait_ge(mix_lo, at(mix_lo, layer, NT))
                pe.wait_ge(mod_done, at(mod_done, layer, MOD_ALL))
                pe.wait_ge(ones_set, at(ones_set, layer, 2))
                pe.wait_ge(v_moved, at(v_moved, layer, PER[v_moved]))
                for i in range(NU + 6):
                    if i < NU:
                        na_scores(i, layer)
                    if 2 <= i < NU + 2:
                        na_transposes(i - 2, layer)
                    if 3 <= i < NU + 3:
                        na_values(i - 3, layer)
                    if i % 8 == 4 and i >= 8:
                        jb = i // 8 - 1
                        pe.wait_ge(na_o, at(na_o, layer, 2 * jb + 2))
                        pe.wait_ge(mix_lo, at(mix_lo, layer, NT + jb))
                        for a in range(HP):
                            i_ = pe.transpose(bank[7][:, a * P:(a + 1) * P], on[:, jb % 2, a * P:(a + 1) * P], ident[:])
                        i_.then_inc(mix_tp, 1)
                layer = stage(pe, the_layer)
                pe.wait_ge(mix_lo, at(mix_lo, layer, 2 * NT))
                gate_rows(0, layer)
                for q in range(4):
                    g = W_OUT0 + q
                    pe.wait_ge(*freed(stream_of(g), layer))
                    for tt in range(NT):
                        if q == 0 and tt == 4:
                            pe.wait_ge(gb_done, at(gb_done, layer, 4))
                        tok = slice(tt * P, (tt + 1) * P)
                        for kk in range(2):
                            k = 2 * q + kk
                            i_ = mm3(bank[tt][:], aT_hi[:, k, tok], aT_lo[:, k, tok],
                                     w_hi[:, g % 4, kk * W:(kk + 1) * W], w_lo[:, g % 4, kk * W:(kk + 1) * W],
                                     k == 0, k == KD - 1)
                        if tt == NT - 1:
                            i_.then_inc(w_used, 1)
                        elif q == 3:
                            i_.then_inc(y_done, 1)
                for tt in range(NT):
                    tok = slice(tt * P, (tt + 1) * P)
                    if tt >= 3:
                        pe.wait_ge(y_copied, at(y_copied, layer, tt - 2))
                        pe.wait_ge(y_sq, at(y_sq, layer, tt - 2))
                    for q in range(4):
                        g = W_OUT0 + 4 + q
                        if tt == 0:
                            pe.wait_ge(*freed(stream_of(g), layer))
                        for kk in range(2):
                            k = 2 * q + kk
                            i_ = mm3(bank[out_bank[1][tt]][:], aT_hi[:, k, tok], aT_lo[:, k, tok],
                                     w_hi[:, g % 4, kk * W:(kk + 1) * W], w_lo[:, g % 4, kk * W:(kk + 1) * W],
                                     k == 0, k == KD - 1)
                        if tt == NT - 1:
                            i_.then_inc(w_used, 1)
                    if tt < NT - 1:
                        i_.then_inc(y_done, 1)
                layer = stage(pe, the_layer)
                pre_norm_tp(1, layer)
                with pe.Fori(0, KF // 2) as j:
                    pe.wait_ge(norm_lo, at(norm_lo, layer, 2 * KD))
                    for c in range(4):
                        pe.wait_ge(raw_free[c], at(raw_free[c], layer, j + (S_UP0 // 4 + 1)))
                        pe.wait_ge(conv_done, at(conv_done, layer, 4 * j + c - 3))
                        for k in range(KD):
                            wh, wl = w_hi[:, c, k * P:(k + 1) * P], w_lo[:, c, k * P:(k + 1) * P]
                            outs = ((bank[c][:], slice(CTX, TOK)), (bank[4 + c][:, 0:CTX], slice(0, CTX)))
                            for out, tok in outs:
                                pe.matmul(out, wl, aT_hi[:, k, tok], start=k == 0, stop=False)
                            for out, tok in outs:
                                pe.matmul(out, wh, aT_lo[:, k, tok], start=False, stop=False)
                            for out, tok in outs:
                                i_ = pe.matmul(out, wh, aT_hi[:, k, tok], start=False, stop=k == KD - 1)
                        i_.then_inc(w_used, 1)
                pe.wait_ge(conv_done, at(conv_done, layer, G_UP))
                gate_rows(1, layer)
                layer = stage(pe, the_layer)
                with pe.Fori(0, 2) as n:
                    for i, kts in enumerate(DOWN_KT):
                        s = W_DOWN0 + i + ADA
                        pe.wait_ge(raw_free[s % 4], at(raw_free[s % 4], layer, 3 * n + (s // 4 + 1)))
                        pe.wait_ge(mlo_done, at(mlo_done, layer, KF * n + (kts[-1] + 1)))
                        for tt in range(NT):
                            if i == 0:
                                pe.wait_ge(y_copied, at(y_copied, layer, NT * n + (tt + 1)))
                                pe.wait_ge(y_sq, at(y_sq, layer, NT * n + (NT + tt + 1)))
                            if i == 0 and tt == 4:
                                pe.wait_ge(gb_done, at(gb_done, layer, 8))
                            for kk, kt in enumerate(kts):
                                q = kt % 4
                                tok = slice(tt * P, (tt + 1) * P)
                                i_ = mm3(bank[tt][:], m_hi[:, q, tok], m_lo[:, q, tok],
                                         w_hi[:, i % 4, kk * W:(kk + 1) * W], w_lo[:, i % 4, kk * W:(kk + 1) * W],
                                         kt == 0, kt == KF - 1)
                            if tt == NT - 1:
                                i_.then_inc(w_used, 1)
                            elif i == len(DOWN_KT) - 1:
                                i_.then_inc(y_done, 1)


def bind(nc, arrays, outs):
    a = {n: nc.dram_tensor("in_" + n, v.shape, mybir.dt.from_np(v.dtype), kind="ExternalInput").ap() for n, v in arrays.items()}
    for n, shape in outs.items():
        a[n] = nc.dram_tensor("out_" + n, shape, F32, kind="ExternalOutput").ap()
    return a


def constants():
    f = np.float32
    inv = np.power(f(10000.0), -np.arange(0, 32, 2, dtype=f) / f(32))
    pos = np.arange(LAT)
    cos = np.zeros((LAT, 2, 2, 16), f)
    sin = np.zeros((LAT, 2, 2, 16), f)
    for g, p in enumerate((pos // GRID_W, pos % GRID_W)):
        ang = p[:, None].astype(f) * inv[None, :]
        cos[:, g] = np.cos(ang)[:, None]
        sin[:, g, 0], sin[:, g, 1] = -np.sin(ang), np.sin(ang)
    rope = np.stack([cos.reshape(LAT, DH), sin.reshape(LAT, DH)])
    rope = rope.reshape(2, NT - 1, P, DH).transpose(2, 0, 1, 3)
    p = np.arange(P)
    dist = np.arange(DIST)[None, :] - 3 * P - p[:, None]
    i = np.arange(LAT)
    qpos = np.broadcast_to(np.stack([i + 1, LAT - i])[None], (P, 2, LAT))
    kpos = np.stack([P - 1 - p, p], 1)
    c, k = p[:, None] % CB, np.arange(CB)[None, :]
    half = CB // 2
    ok = np.stack([k < c + half,
                   k - CB >= c - half,
                   (k >= c - half) & (k < c + half),
                   k + CB < c + half,
                   k >= c - half], 1)
    masks = np.where(ok, 0.0, NEG)
    return {n: np.ascontiguousarray(v, dtype=f) for n, v in
            dict(ident=np.eye(P), rope=rope, dist=dist, qpos=qpos, kpos=kpos, masks=masks).items()}


def layout(inp):
    a = constants()
    f = np.float32
    a["xp"], a["xs"] = inp["x_prompt"][0], inp["x_sample"][0]
    a["cond"] = np.stack([inp["c_ctx"], inp["c"][0]]).reshape(2, KD, P).transpose(2, 0, 1)
    par = np.zeros((DEPTH, NPAR, P), f)
    stream = np.zeros((DEPTH, GS, P, 1024), f)
    for l in range(DEPTH):
        par[l] = np.concatenate([np.asarray(inp[n][l]).reshape(-1, P) for n in
                                 ("conv_w", "conv_b", "ada_b", "g_pre_mix", "g_pre_ffn", "g_post_mix", "g_post_ffn")])
        cols = lambda w, c: w[:, c:c + P].reshape(KD, P, P).transpose(1, 0, 2).reshape(P, 1024)
        rows = lambda w, r, n, c: w[r * P:(r + n) * P, c:c + W].reshape(n, P, W).transpose(1, 0, 2).reshape(P, n * W)
        for j in range(ADA_FIRST):
            stream[l, j] = cols(inp["ada_w"][l], j * P)
        for b in range(NB_IN):
            for q in range(4):
                stream[l, stream_in(b, q)] = rows(inp["w_in"][l], 2 * q, 2, W_IN_COL[b] * W)
                stream[l, stream_ada(b, q)] = cols(inp["ada_w"][l], (ADA_FIRST + 4 * b + q) * P)
        for n in range(2):
            for q in range(4):
                stream[l, S_OUT0 + 4 * n + q] = rows(inp["w_out"][l], 2 * q, 2, n * W)
            for i, kts in enumerate(DOWN_KT):
                stream[l, S_DOWN0 + len(DOWN_KT) * n + i, :, 0:len(kts) * W] = rows(inp["w_down"][l], kts[0], len(kts), n * W)
        for j in range(KF):
            for g in range(2):
                stream[l, S_UP0 + 2 * j + g] = cols(inp["w_up"][l], (g * KF + j) * P)
    a["par"] = par.transpose(0, 2, 1)
    a["stream"] = stream.reshape(DEPTH * ROUNDS, SLOTS, P, 1024).transpose(1, 0, 2, 3)
    a["dec_f"], a["dec_b"] = inp["ret_decay_fwd"], inp["ret_decay_bwd"]
    st = np.stack([inp["state_ret_fwd"][0], inp["state_ret_bwd"][0]])
    a["st0"] = st.reshape(2, DEPTH, HP, 2, DH, DH).transpose(1, 3, 4, 0, 2, 5).reshape(DEPTH, P, 2 * HP * DH)
    a["ctx_kT"] = np.asarray(inp["cache_na_k"])[0].reshape(DEPTH, P, HP, P).transpose(0, 3, 2, 1).reshape(DEPTH, P, HP * P)
    a["ctx_v"] = inp["cache_na_v"][0]
    pad = np.zeros((DEPTH, H, 15, 63), f)
    pad[:, :, :, CB:CB + 31] = inp["na_rpb"]
    win = np.zeros((DEPTH, P, H, ROWS, 3 * CB), f)
    for r in range(ROWS):
        for c in range(CB):
            win[:, r * CB + c] = pad[:, :, 7 - r:15 - r, 15 - c:63 - c]
    a["bias"] = win.reshape(DEPTH, P, H * ROWS * 3 * CB)
    return {n: np.ascontiguousarray(v) for n, v in a.items()}


OUTS = {"yp": (CTX, D), "ys": (LAT, D), "nk": (DEPTH, P, W), "nv": (DEPTH, P, W), "st": (DEPTH, P, H * DH)}


def kernel(**inputs):
    import concourse.bacc as bacc
    from concourse.bass_utils import run_bass_kernel_spmd

    nc = bacc.Bacc("TRN2", target_bir_lowering=False, num_devices=1, dynamic_dma_scratch_size=1024)
    arrays = layout({n: np.asarray(v) for n, v in inputs.items()})
    build(nc, bind(nc, arrays, OUTS))
    r = run_bass_kernel_spmd(nc, [{"in_" + n: v for n, v in arrays.items()}], core_ids=[0]).results[0]
    r = {n: r["out_" + n] for n in OUTS}
    st = r["st"].reshape(DEPTH, 2, DH, H, DH).transpose(1, 0, 3, 2, 4)
    nk, nv = (r[n].reshape(1, DEPTH, P, H, DH) for n in ("nk", "nv"))
    return r["yp"][None], r["ys"][None], nk, nv, st[0][None], st[1][None]
```

```python
from contextlib import ExitStack

import numpy as np

import concourse.bass as bass
from concourse import mybir

F32 = mybir.dt.float32
F32R = mybir.dt.float32r
F16 = mybir.dt.float16
ACT = mybir.ActivationFunctionType
ALU = mybir.AluOpType
AX = mybir.AxisListType

P = 128
D = 1024
DEPTH = 2
CTX = 128
LAT = 512
TOK = CTX + LAT
NT = TOK // P
TH = TOK // 2
GRID_W = 64
ROWS = LAT // GRID_W
DH = 64
H = 8
HP = H // 2
F = 2816
KD = D // P
KF = F // P
W = 512
NB_IN = 7
W_IN_COL = [0, 1, 2, 3, 6, 4, 5]
EPS = 1e-6
NEG = -1e9
BIG = 3.0e38
SCALE = DH ** -0.5
CB = 16
NQB = GRID_W // CB
DIST = 7 * P

SLOTS = 4
ADA = 6 * KD
ADA_FIRST = 2 * KD
G_IN = NB_IN * 4
G_OUT = 2 * 4
G_UP = 2 * KF
DOWN_KT = [(2 * i, 2 * i + 1) for i in range(10)] + [(20,), (21,)]
G_DOWN = 2 * len(DOWN_KT)
GW = G_IN + G_OUT + G_UP + G_DOWN
BIAS_ROUND = 12
GS = ADA + GW
ROUNDS = GS // SLOTS
W_OUT0 = G_IN
W_UP0 = W_OUT0 + G_OUT
W_DOWN0 = W_UP0 + G_UP
LEAD_ROUNDS = ADA_FIRST // SLOTS
S_OUT0 = NB_IN * 8
S_UP0 = S_OUT0 + G_OUT + 4
S_DOWN0 = S_UP0 + G_UP
S_HALF = (G_DOWN + ADA_FIRST) // 2
assert GS % SLOTS == 0 and GW % SLOTS == 0 and S_HALF % SLOTS == 0 and S_DOWN0 + 2 * S_HALF == GS
assert S_UP0 % SLOTS == 0 and W_UP0 % SLOTS == 0 and ADA_FIRST + 4 * NB_IN + 4 == ADA


def stream_in(b, q):
    return 8 * b + (q if q < 2 else q + 2)


def stream_out(q):
    return S_OUT0 + q + 2 * min(q // 2, 2)


def stream_down(q):
    n, i = divmod(q, len(DOWN_KT))
    return S_DOWN0 + S_HALF * n + (i if i < 4 else 2 * i - 3)


def stream_ada(col):
    if col < ADA_FIRST:
        n, i = divmod(col, ADA_FIRST // 2)
        return S_DOWN0 + S_HALF * n + 4 + 2 * i
    b, q = divmod(col - ADA_FIRST, 4)
    return 8 * b + (q + 2 if q < 2 else q + 4)


C_TAP, C_CB, C_AB, C_GM, C_GF, C_PM, C_PF = 0, 132, 176, 224, 232, 240, 248
NPAR = 256

UNITS = [(jb, h) for jb in range(NQB + 1) for h in range(H)]
NBIAS = 5


def key_blocks(jb):
    if jb == NQB:
        return [], 0
    if jb == 0:
        return [1, 0], 3
    if jb == NQB - 1:
        return [NQB - 1, NQB - 2], 0
    return [jb - 1, jb, jb + 1], 1


def build(nc, t):
    with ExitStack() as ctx:
        def sem(name):
            return ctx.enter_context(nc.semaphore(name))

        def sb(name, shape, dt=F32, stack=ctx):
            return stack.enter_context(nc.sbuf_tensor(name, shape, dt))

        x = sb("x", [P, NT, D])
        raw = sb("raw", [P, SLOTS, 1024])
        w_hi = sb("w_hi", [P, SLOTS, 1024], F32R)
        w_lo = sb("w_lo", [P, SLOTS, 1024], F32R)
        ident = sb("ident", [P, P])
        rope = sb("rope", [P, 2, NT - 1, DH])
        dist = sb("dist", [P, DIST], F16)
        qpos = sb("qpos", [P, 2, LAT], F16)
        kpos = sb("kpos", [P, 2])
        masks = sb("masks", [P, NBIAS, CB])
        cond = sb("cond", [P, 2, D])
        ada_sq = sb("ada_sq", [P, D])
        par = sb("par", [P, NPAR])
        mod = sb("mod", [P, ADA, 2])
        dec = sb("dec", [P, 2, H])
        lgt = sb("lgt", [P, 4, 2 * H])
        lg = sb("lg", [P, 2, H])
        nlg = sb("nlg", [P, H])
        lgp = sb("lgp", [P, 2, HP])
        kdec = sb("kdec", [P, 2, H])
        st0 = sb("st0", [P, 2, HP, DH])
        ctx_kT = sb("ctx_kT", [P, HP, P])
        ctx_v = sb("ctx_v", [P, H, DH])
        ssq = sb("ssq", [P, 2, NT])
        base = sb("base", [P, NT])
        std = sb("std", [P, NT])
        rstd = sb("rstd", [P, NT])
        eps = sb("eps", [P, 1])
        prime = sb("prime", [P, 16])
        gn = sb("gn", [P, 4, NT, H])
        nmax = sb("nmax", [P, 4])
        cmax = sb("cmax", [P, 4, 2])
        esum = sb("esum", [P, 4, 2])
        rec = sb("rec", [P, 4])

        with ExitStack() as s:
            m_hi = sb("m_hi", [P, 4, TOK], F32R, s)
            m_lo = sb("m_lo", [P, 4, TOK], F32R, s)
        aT_hi = sb("aT_hi", [P, KD, TOK], F32R)
        with ExitStack() as s:
            y_ffn = sb("y_ffn", [P, NT, W], F32, s)
            zt_ffn = sb("zt_ffn", [P, D], F32, s)
        aT_lo = sb("aT_lo", [P, KD, TOK], F32R)

        with ExitStack() as s:
            qT = sb("qT", [P, HP, TOK], F32, s)
            with ExitStack() as s2:
                xc = sb("xc", [P, NT, W], F32, s2)
            with ExitStack() as s2:
                vn = sb("vn", [P, NT, W], F32, s2)
            kT = sb("kT", [P, HP, TOK], F32, s)
            vt = sb("vt", [P, NT, H, DH], F32, s)
            sg = sb("sg", [P, NT, W], F32, s)
            with ExitStack() as s2:
                xsq = sb("xsq", [P, NT, W], F32, s2)
            with ExitStack() as s2:
                t1 = sb("t1", [P, 2, W], F32, s2)
            with ExitStack() as s2:
                toe = sb("toe", [P, 2, DIST], F32, s2)
                qf = sb("qf", [P, 2, 2, LAT], F32, s2)
                pr = sb("pr", [P, 4, LAT], F32, s2)
                kp = sb("kp", [P, H, DH], F32, s2)
                kd = sb("kd", [P, 2, H, DH], F32, s2)
            with ExitStack() as s2:
                bias_raw = sb("bias_raw", [P, H * ROWS, 3 * CB], F32, s2)
                bias = sb("bias", [P, H, NBIAS, P], F32, s2)
                stt = sb("stt", [P, W], F32, s2)
                with ExitStack() as s3:
                    oT = sb("oT", [P, HP, TOK], F32, s3)
                with ExitStack() as s3:
                    tm = sb("tm", [P, NT, W], F32, s3)
                sp = sb("sp", [P, 4, W], F32, s2)
                pt = sb("pt", [P, 2, W], F32, s2)
        with ExitStack() as s:
            diag = sb("diag", [P, NT, P], F32, s)
            tf = sb("tf", [P, 2, TOK], F32, s)
            y_mix = sb("y_mix", [P, NT, W], F32, s)
            zt = sb("zt", [P, D], F32, s)
            gb_mix = sb("gb_mix", [P, 2, D], F32, s)
            sq_mix = sb("sq_mix", [P, D], F32, s)
        with ExitStack() as s:
            m = sb("m", [P, KF, TOK], F32, s)
            cv = sb("cv", [P, 4, TOK], F32, s)
            gb_ffn = sb("gb_ffn", [P, 2, D], F32, s)
            sq_ffn = sb("sq_ffn", [P, W], F32, s)

        bank = [ctx.enter_context(nc.psum_tensor(f"bank{i}", [P, 512], F32)) for i in range(8)]
        CTX_BANK = (4, 7)


        PER, PRIME, LEAD = {}, {}, {}

        def counted(name, per, prime=0, lead=0):
            s_ = sem(name)
            PER[s_], PRIME[s_], LEAD[s_] = per, prime, lead
            return s_

        cond_in = sem("cond_in")
        const_in = sem("const_in")
        y_out = sem("y_out")
        cond_silu = sem("cond_silu")
        raw_full = [counted(f"raw_full{i}", 16 * ROUNDS, 0, 16 * LEAD_ROUNDS) for i in range(SLOTS)]
        raw_free = [counted(f"raw_free{i}", ROUNDS, 1, LEAD_ROUNDS) for i in range(SLOTS)]
        ada_part = counted("ada_part", ADA, 0, ADA_FIRST)
        hi_done = counted("hi_done", GW)
        w_used = counted("w_used", GW, 4)
        par_in = counted("par_in", 16 * 6)
        bias_in = counted("bias_in", 16)
        kv_out = counted("kv_out", 16 * 3)
        v_moved = counted("v_moved", 16 * (1 + ROWS * NQB))
        mod_done = counted("mod_done", 5)
        lg_step = counted("lg_step", 19)
        lg_exp = counted("lg_exp", 1)
        kdec_done = counted("kdec_done", 1)
        pre_sq = counted("pre_sq", 2 * NT)
        pre_std = counted("pre_std", 2 * NT)
        pre_rstd = counted("pre_rstd", 2 * NT)
        diag_done = counted("diag_done", 2 * NT)
        norm_tp = counted("norm_tp", 2 * KD)
        norm_mod = counted("norm_mod", 2 * KD)
        norm_hi = counted("norm_hi", 2 * KD)
        norm_lo = counted("norm_lo", 2 * KD)
        in_done = counted("in_done", NB_IN * (NT - 1))
        rope_part = counted("rope_part", 2 * 4 * 3)
        rope_done = counted("rope_done", 2 * NT)
        in_copied = counted("in_copied", 5 * NT)
        qk_tp = counted("qk_tp", 4 * NT)
        qk_T = counted("qk_T", 4 * NT)
        kp_done = counted("kp_done", 1)
        kd_done = counted("kd_done", 1)
        toe_lin = counted("toe_lin", H)
        toe_min = counted("toe_min", H)
        toe_exp = counted("toe_exp", H)
        toe_done = counted("toe_done", H)
        qf_exp = counted("qf_exp", HP)
        qf_done = counted("qf_done", HP)
        ret_s = counted("ret_s", 5 * H)
        ret_p = counted("ret_p", 5 * H)
        ret_av = counted("ret_av", 5 * H)
        ret_oT = counted("ret_oT", HP + 1)
        ret_tp = counted("ret_tp", NT)
        st_mm = counted("st_mm", 1)
        st_done = counted("st_done", 1)
        gn_read = counted("gn_read", NT)
        gn_step = counted("gn_step", 5 * NT)
        gn_sq = counted("gn_sq", NT)
        gn_std = counted("gn_std", NT)
        ret_done = counted("ret_done", NT)
        bias_done = counted("bias_done", NBIAS)
        mix_tp = counted("mix_tp", NT)
        mix_hi = counted("mix_hi", 2 * NT)
        mix_lo = counted("mix_lo", 2 * NT)
        NU = len(UNITS)
        na_s = counted("na_s", NU)
        na_c = counted("na_c", NQB * H)
        na_m = counted("na_m", NU)
        na_e = counted("na_e", NU)
        na_t = counted("na_t", NU)
        na_p = counted("na_p", NU)
        na_av = counted("na_av", NU)
        na_r = counted("na_r", 2 * NQB * H + H)
        na_d = counted("na_d", NU)
        gb_mm = counted("gb_mm", 8)
        gb_done = counted("gb_done", 8)
        y_done = counted("y_done", 4 * (NT - 1))
        y_sq = counted("y_sq", 4 * NT)
        y_copied = counted("y_copied", 2 * NT)
        y_base = counted("y_base", 2)
        post_std = counted("post_std", 2 * NT)
        post_rstd = counted("post_rstd", 2 * NT)
        post_y = counted("post_y", 4 * NT)
        x_done = counted("x_done", 2 * NT, 2 * NT)
        tap_mid = counted("tap_mid", G_UP)
        tap_left = counted("tap_left", 3 * G_UP)
        conv_done = counted("conv_done", G_UP, 4)
        silu_done = counted("silu_done", KF)
        m_done = counted("m_done", KF, 2)
        mhi_done = counted("mhi_done", 2 * KF)
        mlo_done = counted("mlo_done", 2 * KF)
        primed = sem("primed")

        block = ctx.enter_context(nc.Block())

        def stage(eng, layer):
            reg = eng.alloc_register()
            eng.reg_mov(reg, layer)
            return eng.snap(reg, min_val=0, max_val=DEPTH - 1)

        def at(s_, layer, n):
            return layer * PER[s_] + (n + PRIME[s_] + LEAD[s_])

        def full(s, layer):
            return raw_full[s % SLOTS], at(raw_full[s % SLOTS], layer, 16 * (s // SLOTS + 1))

        def freed(s, layer):
            return raw_free[s % SLOTS], at(raw_free[s % SLOTS], layer, s // SLOTS + 1)

        def stream_of(g):
            if g < W_OUT0:
                return stream_in(g // 4, g % 4)
            if g < W_UP0:
                return stream_out(g - W_OUT0)
            return g - W_UP0 + S_UP0 if g < W_DOWN0 else stream_down(g - W_DOWN0)

        halves = [(DH * (h % 2), h // 2) for h in range(H)]

        def in_bank(b, tt):
            return (NT * b + tt) % 7

        def qk_bank(b, tt):
            return (NT * (b + 2) + tt % 2) % 7

        qk_blocks = [0, 1, 5, 6]
        GB_BANKS = [5, 6, 7, 4]
        MIX_BANKS = [3, 4, 5, 6, 3]
        NA_BANKS = [0, 1, 2, 7]
        RET_BANKS = [5, 6, 7, 2, 3]
        out_bank = [[0, 1, 2, 3, 4], [5, 6, 7, 0, 1]]

        @block.sync
        def _(sp_):
            sp_.dma_start(cond[:].rearrange("p c d -> p (c d)"), t["cond"].to_broadcast([P, 2 * D])).then_inc(cond_in, 16)
            sp_.wait_ge(primed, 1)

            def stream(layer, first, last):
                with sp_.Fori(first, last) as r:
                    rnd = r if layer is None else sp_.snap(layer * ROUNDS + r + LEAD_ROUNDS)
                    for s in range(SLOTS):
                        src = t["stream"][s, bass.ds(rnd, 1), :, :].rearrange("o p n -> p (o n)")
                        sp_.wait_ge(raw_free[s], rnd + 1)
                        sp_.dma_start(raw[:, s, :], src).then_inc(raw_full[s], 16)

            stream(None, 0, 1)
            for dst, src in [(ident[:], t["ident"]), (rope[:], t["rope"]), (dist[:], t["dist"]), (qpos[:], t["qpos"]),
                             (kpos[:], t["kpos"]), (masks[:], t["masks"]),
                             (x[:, 0, :], t["xp"]), (x[:, 1:NT, :], t["xs"].rearrange("(i p) d -> p i d", p=P))]:
                sp_.dma_start(dst, src).then_inc(const_in, 16)
            stream(None, 1, LEAD_ROUNDS)
            with sp_.Fori(0, DEPTH) as layer:
                lay = bass.ds(layer, 1)
                for dst, src in [(par[:], t["par"][lay].rearrange("o p n -> p (o n)")),
                                 (dec[:, 0, :], t["dec_f"][lay].to_broadcast([P, H])),
                                 (dec[:, 1, :], t["dec_b"][lay].to_broadcast([P, H])),
                                 (st0[:], t["st0"][lay].rearrange("o p n -> p (o n)")),
                                 (ctx_kT[:], t["ctx_kT"][lay].rearrange("o p n -> p (o n)")),
                                 (ctx_v[:, :, 0:DH], t["ctx_v"][lay].rearrange("o p h d -> (o p) h d"))]:
                    sp_.dma_start(dst, src).then_inc(par_in, 16)
                stream(layer, 0, BIAS_ROUND)
                sp_.dma_start(bias_raw[:], t["bias"][lay].rearrange("o p n -> p (o n)")).then_inc(bias_in, 16)
                sp_.wait_ge(st_done, at(st_done, layer, 1))
                sp_.dma_start(t["st"][lay].rearrange("o p n -> (o p) n"), stt[:]).then_inc(kv_out, 16)
                sp_.wait_ge(in_copied, at(in_copied, layer, 3 * NT))
                sp_.dma_start(t["nv"][lay].rearrange("o p n -> (o p) n"), vn[:, 0, :]).then_inc(kv_out, 16)
                sp_.dma_start(vt[:, 0, :, 0:DH], vn[:, 0, :].rearrange("p (h d) -> p h d", h=H)).then_inc(v_moved, 16)
                for r in range(ROWS):
                    tt, p0 = 1 + r // 2, GRID_W * (r % 2)
                    for jb in range(NQB):
                        sp_.dma_start(vt[CB * r:CB * (r + 1), 1 + jb, :, 0:DH],
                                      vn[p0 + CB * jb:p0 + CB * (jb + 1), tt, :].rearrange("p (h d) -> p h d", h=H)
                                      ).then_inc(v_moved, 16)
                stream(layer, BIAS_ROUND, BIAS_ROUND + 4)
                sp_.wait_ge(in_copied, at(in_copied, layer, 4 * NT + 1))
                sp_.dma_start(t["nk"][lay].rearrange("o p n -> (o p) n"), tm[:, 0, :]).then_inc(kv_out, 16)
                stream(layer, BIAS_ROUND + 4, ROUNDS)
            for tt in range(NT):
                sp_.wait_ge(x_done, DEPTH * 2 * NT + NT + tt + 1)
                dst = t["yp"] if tt == 0 else t["ys"][(tt - 1) * P:tt * P, :]
                sp_.dma_start(dst, x[:, tt, :]).then_inc(y_out, 16)
            sp_.wait_ge(y_out, 16 * NT)
            sp_.wait_ge(kv_out, 16 * 3 * DEPTH)

        @block.gpsimd
        def _(pool):
            for n, (s_, k) in enumerate((s_, k) for s_, k in PRIME.items() if k):
                pool.memset(prime[:, n:n + 1], 0.0).then_inc(s_, k)
            pool.memset(eps[:], EPS).then_inc(primed, 1)
            with pool.Fori(0, DEPTH) as layer:
                pool.wait_ge(bias_in, at(bias_in, layer, 16))
                for e_, part in enumerate([1, 0, 1, 2, 1]):
                    pool.tensor_tensor(
                        bias[:, :, e_, :].rearrange("p h (r c) -> p h r c", c=CB),
                        bias_raw[:].rearrange("p (h r) k -> p h r k", h=H)[:, :, :, part * CB:(part + 1) * CB],
                        masks[:, e_, :].unsqueeze(1).unsqueeze(1).to_broadcast([P, H, ROWS, CB]),
                        ALU.add).then_inc(bias_done, 1)

        MOD_PRE, MOD_ALL = 2, 5
        LG_ABS, LG_ALL = 2, 19

        def tile_done(b, tt, layer):
            if tt < NT - 1:
                return in_done, at(in_done, layer, (NT - 1) * b + tt + 1)
            return w_used, at(w_used, layer, 4 * b + 4)

        def half_done(w, n, tt, layer):
            if tt < NT - 1:
                return y_done, at(y_done, layer, (NT - 1) * (2 * w + n) + tt + 1)
            last = W_DOWN0 + len(DOWN_KT) * (n + 1) if w else W_OUT0 + 4 * (n + 1)
            return w_used, at(w_used, layer, last)

        def kt_free(q, layer):
            n, kt = divmod(q, KF)
            if n == 0 and kt < 4:
                return at(w_used, layer, W_DOWN0)
            if kt >= 4:
                kt -= 4
            else:
                n, kt = 0, max(k for k in range(KF) if k % 4 == kt)
            gi = next(i for i, kts in enumerate(DOWN_KT) if kt in kts)
            return at(w_used, layer, W_DOWN0 + len(DOWN_KT) * n + gi + 1)

        def x_ready(w, tt, layer):
            return at(x_done, layer, NT * w + tt + 1 - NT)

        def width(g):
            return 512 if g >= W_DOWN0 and (g - W_DOWN0) % len(DOWN_KT) >= 10 else 1024

        def blk(ap):
            return ap.rearrange("p (a q) -> p a q", a=4)

        def grid(ap, jb):
            return ap.rearrange("p (r c) -> p r c", c=GRID_W)[:, :, CB * jb:CB * (jb + 1)]

        def tap(i, c, j):
            return par[:, bass.ds(2 * j + (C_TAP + (i * 2 + c % 2) * KF + c // 2), 1)]

        @block.scalar
        def _(act):
            act.wait_ge(cond_in, 16)
            act.activation(cond[:], cond[:], ACT.Silu).then_inc(cond_silu, 1)
            act.wait_ge(const_in, 16 * 8)
            act.wait_ge(primed, 1)

            def split_hi(g, layer):
                s, n = stream_of(g), width(g)
                act.wait_ge(*full(s, layer))
                act.wait_ge(w_used, at(w_used, layer, g - 3))
                act.activation(w_hi[:, g % 4, 0:n], raw[:, s % 4, 0:n], ACT.Copy).then_inc(hi_done, 1)

            def pre_norm(w, layer):
                for tt in range(NT):
                    i = NT * w + tt
                    act.wait_ge(x_done, x_ready(w, tt, layer))
                    act.activation(sq_mix[:], x[:, tt, :], ACT.Square, accum_out=ssq[:, 0, tt:tt + 1]).then_inc(pre_sq, 1)
                    act.wait_ge(pre_sq, at(pre_sq, layer, i + 1))
                    act.activation(std[:, tt:tt + 1], ssq[:, 0, tt:tt + 1], ACT.Sqrt, bias=eps[:],
                                   scale=1.0 / D).then_inc(pre_std, 1)
                first = W_UP0 if w else 0
                for g in range(first, first + 2):
                    split_hi(g, layer)
                for k in range(KD):
                    i = KD * w + k
                    act.wait_ge(norm_mod, at(norm_mod, layer, i + 1))
                    act.activation(aT_hi[:, k, :], tf[:, k % 2, :], ACT.Copy).then_inc(norm_hi, 1)
                for g in range(first + 2, first + 4):
                    split_hi(g, layer)

            def toe_table(h, layer):
                if h >= 2:
                    act.wait_ge(ret_p, at(ret_p, layer, 5 * (h - 1)))
                act.activation(toe[:, h % 2, :], dist[:], ACT.Copy, scale=lg[:, 0, h:h + 1]).then_inc(toe_lin, 1)
                act.wait_ge(toe_min, at(toe_min, layer, h + 1))
                act.activation(toe[:, h % 2, :], toe[:, h % 2, :], ACT.Exp).then_inc(toe_exp, 1)

            def query_decay(a, layer):
                if a >= 2:
                    act.wait_ge(ret_av, at(ret_av, layer, 10 * (a - 1)))
                act.activation(qf[:, a % 2, 0, :], qpos[:, 0, :], ACT.Exp, scale=lgp[:, 0, a:a + 1])
                act.activation(qf[:, a % 2, 1, :], qpos[:, 1, :], ACT.Exp,
                               scale=lgp[:, 1, a:a + 1]).then_inc(qf_exp, 1)

            def pair_out(a, layer):
                act.wait_ge(ret_av, at(ret_av, layer, 10 * (a + 1)))
                act.activation(oT[:, a, 0:LAT], bank[a % 2][:], ACT.Copy).then_inc(ret_oT, 1)

            def qk_evac(b, layer):
                dst = qT if b in (0, 5) else kT
                scale = SCALE if b in (0, 5) else 1.0
                if b == 6:
                    act.wait_ge(v_moved, at(v_moved, layer, PER[v_moved]))
                    act.wait_ge(kv_out, at(kv_out, layer, 32))
                for tt in range(NT):
                    act.wait_ge(qk_tp, at(qk_tp, layer, NT * qk_blocks.index(b) + tt + 1))
                    src = blk(bank[qk_bank(b, tt)][:])
                    if b < 2 or tt == 0:
                        act.activation(dst[:, :, tt * P:(tt + 1) * P], src, ACT.Copy, scale=scale).then_inc(qk_T, 1)
                        continue
                    for i in range(2):
                        i_ = act.activation(
                            dst[:, :, P:TOK].rearrange("p a (j r c) -> p a j r c", j=NQB, r=ROWS)[:, :, :, 2 * tt - 2 + i, :],
                            src.rearrange("p a (i j c) -> p a i j c", i=2, j=NQB)[:, :, i, :, :], ACT.Copy, scale=scale)
                    i_.then_inc(qk_T, 1)

            def gate_rows(w, layer):
                gb = gb_ffn if w else gb_mix
                for i in range(4):
                    act.wait_ge(gb_mm, at(gb_mm, layer, 4 * w + i + 1))
                    act.activation(gb[:, i // 2, (i % 2) * W:(i % 2 + 1) * W], bank[GB_BANKS[i]][:],
                                   ACT.Copy).then_inc(gb_done, 1)

            def half_squares(w, n, layer):
                for tt in range(NT):
                    b = tt if w else out_bank[n][tt]
                    i = 2 * NT * w + NT * n + tt
                    act.wait_ge(*half_done(w, n, tt, layer))
                    act.activation((sq_ffn if w else sq_mix)[:, 0:W], bank[b][:], ACT.Square,
                                   accum_out=ssq[:, n, tt:tt + 1]).then_inc(y_sq, 1)
                    act.wait_ge(y_sq, at(y_sq, layer, i + 1))
                    if n == 1:
                        act.wait_ge(y_base, at(y_base, layer, w + 1))
                        act.activation(std[:, tt:tt + 1], ssq[:, 1, tt:tt + 1], ACT.Sqrt, bias=base[:, tt:tt + 1],
                                       scale=1.0 / D).then_inc(post_std, 1)

            with act.Fori(0, DEPTH) as the_layer:
                layer = stage(act, the_layer)
                pre_norm(0, layer)
                act.wait_ge(lg_step, at(lg_step, layer, LG_ABS))
                act.activation(lgt[:, 2, :], lgt[:, 1, :], ACT.Exp, scale=-1.0).then_inc(lg_exp, 1)
                for b in range(NB_IN):
                    layer = stage(act, the_layer)
                    if b - 1 in qk_blocks:
                        qk_evac(b - 1, layer)
                    for q in range(3):
                        split_hi(4 * (b + 1) + q, layer)
                    if b == 3:
                        act.wait_ge(lg_step, at(lg_step, layer, LG_ALL))
                        for d in range(2):
                            i_ = act.activation(kdec[:, d, :], lg[:, d, :], ACT.Exp, scale=kpos[:, d:d + 1])
                        i_.then_inc(kdec_done, 1)
                        toe_table(0, layer)
                        query_decay(0, layer)
                    for tt in range(NT):
                        if b < 2:
                            break
                        act.wait_ge(*tile_done(b, tt, layer))
                        src = bank[in_bank(b, tt)][:]
                        if b == 3:
                            act.activation(sg[:, tt, :], src, ACT.Silu).then_inc(in_copied, 1)
                            continue
                        if b == 2:
                            act.activation(vt[:, tt, :, 0:DH], src.rearrange("p (h d) -> p h d", h=H),
                                           ACT.Copy).then_inc(in_copied, 1)
                        else:
                            act.activation((vn if b == 4 else tm)[:, tt, :], src, ACT.Copy).then_inc(in_copied, 1)
                    split_hi(4 * (b + 1) + 3, layer)
                    if b == 3:
                        layer = stage(act, the_layer)
                        for h in range(H):
                            if h + 1 < H:
                                toe_table(h + 1, layer)
                            if h % 2 == 0 and h // 2 + 1 < HP:
                                query_decay(h // 2 + 1, layer)
                            if h % 2 and h > 1:
                                pair_out(h // 2 - 1, layer)
                        pair_out(HP - 1, layer)
                        act.activation(oT[:, :, LAT:TOK], blk(bank[4][:]), ACT.Copy).then_inc(ret_oT, 1)
                        for i in range(NT):
                            tt = (i + 1) % NT
                            act.wait_ge(gn_read, at(gn_read, layer, i + 1))
                            act.activation(xsq[:, tt, :], xc[:, tt, :], ACT.Square).then_inc(gn_sq, 1)
                        act.wait_ge(st_mm, at(st_mm, layer, 1))
                        act.activation(stt[:], bank[5][:], ACT.Copy).then_inc(st_done, 1)
                        for i in range(NT):
                            tt = (i + 1) % NT
                            act.wait_ge(gn_step, at(gn_step, layer, 2 * NT + i + 1))
                            act.activation(gn[:, 3, tt, :], gn[:, 2, tt, :], ACT.Sqrt, bias=eps[:],
                                           scale=1.0 / DH).then_inc(gn_std, 1)
                qk_evac(6, layer)
                layer = stage(act, the_layer)
                for tt in range(NT):
                    act.wait_ge(mix_tp, at(mix_tp, layer, tt + 1))
                    act.activation(aT_hi[:, 0:HP, tt * P:(tt + 1) * P], blk(bank[MIX_BANKS[tt]][:]),
                                   ACT.Copy).then_inc(mix_hi, 1)
                layer = stage(act, the_layer)
                for i in range(NU + 6):
                    if i < NU:
                        jb, h = UNITS[i]
                        n = P * len(key_blocks(jb)[0])
                        act.wait_ge(na_m, at(na_m, layer, i + 1))
                        e_ = act.activation(sp[:, i % 4, 0:P], bank[NA_BANKS[i % 4]][:, 0:P], ACT.Exp,
                                            bias=nmax[:, i % 4:i % 4 + 1], accum_out=esum[:, i % 4, 0:1])
                        if n:
                            e_ = act.activation(sp[:, i % 4, P:P + n], sp[:, i % 4, P:P + n], ACT.Exp,
                                                bias=nmax[:, i % 4:i % 4 + 1], scale=-1.0, accum_out=esum[:, i % 4, 1:2])
                        e_.then_inc(na_e, 1)
                    if 2 <= i < NU + 2:
                        u = i - 2
                        n = P * (1 + len(key_blocks(UNITS[u][0])[0]))
                        act.wait_ge(na_t, at(na_t, layer, u + 1))
                        if u >= 2:
                            act.wait_ge(na_av, at(na_av, layer, u - 1))
                        act.activation(pt[:, u % 2, 0:n], bank[3 + u % 2][:, 0:n], ACT.Copy).then_inc(na_p, 1)
                    if i % 8 == 5 and i >= 8:
                        jb = i // 8 - 1
                        act.wait_ge(na_av, at(na_av, layer, H * (jb + 1)))
                        src = blk(bank[5 + jb % 2][:])
                        if jb == NQB:
                            act.activation(aT_hi[:, HP:KD, 0:P], src, ACT.Copy).then_inc(mix_hi, 1)
                        else:
                            for a in range(HP):
                                e_ = act.activation(grid(aT_hi[:, HP + a, P:TOK], jb),
                                                    src[:, a, :].rearrange("p (r c) -> p r c", c=CB), ACT.Copy)
                            e_.then_inc(mix_hi, 1)
                layer = stage(act, the_layer)
                gate_rows(0, layer)
                gate_rows(1, layer)
                for g in range(W_OUT0 + 4, W_OUT0 + 7):
                    split_hi(g, layer)
                half_squares(0, 0, layer)
                split_hi(W_OUT0 + 7, layer)
                half_squares(0, 1, layer)
                layer = stage(act, the_layer)
                pre_norm(1, layer)
                with act.Fori(0, KF // 2) as j:
                    def gate_silu(c):
                        act.wait_ge(conv_done, at(conv_done, layer, 4 * j + c + 1))
                        act.activation(cv[:, c, :], cv[:, c, :], ACT.Silu).then_inc(silu_done, 1)

                    for c in range(4):
                        act.wait_ge(w_used, at(w_used, layer, 4 * j + W_UP0 + c + 1))
                        act.wait_ge(m_done, at(m_done, layer, 2 * j + c // 2 - 1))
                        bias_ = par[:, bass.ds(2 * j + (C_CB + (c % 2) * KF + c // 2), 1)]
                        act.activation(cv[:, c, 0:TH], bank[c][:, 0:TH], ACT.Identity, bias=bias_, scale=tap(1, c, j))
                        act.activation(cv[:, c, TH:TOK], bank[4 + c][:, 0:TH], ACT.Identity, bias=bias_,
                                       scale=tap(1, c, j)).then_inc(tap_mid, 1)
                        act.wait_ge(raw_full[c], at(raw_full[c], layer, 16 * (j + (S_UP0 // 4 + 2))))
                        act.activation(w_hi[:, c, :], raw[:, c, :], ACT.Copy).then_inc(hi_done, 1)
                        if c == 2:
                            gate_silu(1)
                    gate_silu(3)
                layer = stage(act, the_layer)
                for gi in range(G_DOWN):
                    if 2 <= gi and gi + 2 < G_DOWN:
                        split_hi(W_DOWN0 + gi + 2, layer)
                    n, i = divmod(gi, len(DOWN_KT))
                    if gi == len(DOWN_KT):
                        half_squares(1, 0, layer)
                    for kt in DOWN_KT[i]:
                        q = KF * n + kt
                        act.wait_ge(w_used, kt_free(q, layer))
                        act.wait_ge(m_done, at(m_done, layer, kt + 1))
                        act.activation(m_hi[:, kt % 4, :], m[:, kt, :], ACT.Copy).then_inc(mhi_done, 1)
                half_squares(1, 1, layer)

        @block.vector
        def _(dve):
            def split_lo(g, layer):
                s, n = stream_of(g), width(g)
                dve.wait_ge(hi_done, at(hi_done, layer, g + 1))
                dve.tensor_tensor(w_lo[:, g % 4, 0:n], raw[:, s % 4, 0:n], w_hi[:, g % 4, 0:n].bitcast(F32),
                                  ALU.subtract).then_inc(raw_free[s % 4], 1)

            def ada_products(col, src, slot, start):
                dve.tensor_tensor_reduce(ada_sq[:], src, cond[:, 0, :], 1.0, start, ALU.mult, ALU.add,
                                         mod[:, col, 0:1]).then_inc(ada_part, 1)
                dve.tensor_tensor_reduce(src, src, cond[:, 1, :], 1.0, start, ALU.mult, ALU.add,
                                         mod[:, col, 1:2]).then_inc(raw_free[slot], 1)

            def ada(col, layer):
                s = stream_ada(col)
                dve.wait_ge(*full(s, layer))
                n = col - ADA_FIRST if col >= ADA_FIRST else col + ADA - ADA_FIRST
                dve.wait_ge(ada_part, at(ada_part, layer, n))
                ada_products(col, raw[:, s % 4, :], s % 4, 0.0 if col < ADA_FIRST else par[:, C_AB + col:C_AB + col + 1])

            def times_gain(f0, c0, plus):
                return dve.scalar_tensor_tensor(mod[:, f0:f0 + KD, :], mod[:, f0:f0 + KD, :], plus,
                                                par[:, c0:c0 + KD].unsqueeze(2).to_broadcast([P, KD, 2]),
                                                ALU.add, ALU.mult)

            def pre_norm(w, layer):
                for tt in range(NT):
                    i = NT * w + tt
                    dve.wait_ge(pre_std, at(pre_std, layer, i + 1))
                    dve.reciprocal(rstd[:, tt:tt + 1], std[:, tt:tt + 1]).then_inc(pre_rstd, 1)
                    dve.wait_ge(pre_rstd, at(pre_rstd, layer, i + 1))
                    dve.tensor_scalar(diag[:, tt, :], ident[:], rstd[:, tt:tt + 1], None, ALU.mult).then_inc(diag_done, 1)
                if w == 0:
                    dve.tensor_tensor(mod[:, 0:ADA_FIRST, :], mod[:, 0:ADA_FIRST, :],
                                      par[:, C_AB:C_AB + ADA_FIRST].unsqueeze(2).to_broadcast([P, ADA_FIRST, 2]),
                                      ALU.add).then_inc(mod_done, 1)
                    dve.wait_ge(mod_done, at(mod_done, layer, 1))
                    times_gain(KD, C_GM, 1.0).then_inc(mod_done, 1)
                    dve.wait_ge(mod_done, at(mod_done, layer, MOD_PRE))
                else:
                    dve.wait_ge(mod_done, at(mod_done, layer, MOD_ALL))
                sh = 3 * KD * w
                first = W_UP0 if w else 0
                for g in range(first, first + 2):
                    split_lo(g, layer)
                for k in range(KD + 1):
                    i = KD * w + k
                    if k < KD:
                        dve.wait_ge(norm_tp, at(norm_tp, layer, i + 1))
                        if k >= 2:
                            dve.wait_ge(norm_lo, at(norm_lo, layer, i - 1))
                        dve.tensor_scalar(tf[:, k % 2, 0:CTX], bank[CTX_BANK[k % 2]][:, 0:P],
                                          mod[:, sh + KD + k, 0:1], mod[:, sh + k, 0:1], ALU.mult, ALU.add)
                        dve.tensor_scalar(tf[:, k % 2, CTX:TOK], bank[5 + k % 2][:],
                                          mod[:, sh + KD + k, 1:2], mod[:, sh + k, 1:2], ALU.mult,
                                          ALU.add).then_inc(norm_mod, 1)
                    if k >= 1:
                        dve.wait_ge(norm_hi, at(norm_hi, layer, i))
                        dve.tensor_tensor(aT_lo[:, k - 1, :], tf[:, (k - 1) % 2, :], aT_hi[:, k - 1, :].bitcast(F32),
                                          ALU.subtract).then_inc(norm_lo, 1)
                if w == 0:
                    ada(ADA_FIRST, layer)
                    ada(ADA_FIRST + 1, layer)
                for g in range(first + 2, first + 4):
                    split_lo(g, layer)
                if w == 0:
                    ada(ADA_FIRST + 2, layer)
                    ada(ADA_FIRST + 3, layer)

            def decays(layer):
                n = LG_ABS
                lg_in = dec[:].rearrange("p a h -> p (a h)")
                T = [lgt[:, i, :] for i in range(4)]

                def after():
                    dve.wait_ge(lg_step, at(lg_step, layer, n))
                dve.wait_ge(lg_exp, at(lg_exp, layer, 1))
                dve.tensor_scalar(T[0], T[2], 2.0, None, ALU.add).then_inc(lg_step, 1)
                n += 1
                after()
                dve.reciprocal(T[0], T[0]).then_inc(lg_step, 1)
                n += 1
                after()
                dve.tensor_tensor(T[1], T[2], T[0], ALU.mult).then_inc(lg_step, 1)
                n += 1
                after()
                dve.tensor_tensor(T[0], T[1], T[1], ALU.mult).then_inc(lg_step, 1)
                n += 1
                after()
                dve.tensor_scalar(T[3], T[0], 1.0 / 15, None, ALU.mult).then_inc(lg_step, 1)
                n += 1
                for c in (13, 11, 9, 7, 5, 3):
                    after()
                    dve.scalar_tensor_tensor(T[3], T[3], 1.0 / c, T[0], ALU.add, ALU.mult).then_inc(lg_step, 1)
                    n += 1
                after()
                dve.scalar_tensor_tensor(T[3], T[3], 1.0, T[1], ALU.add, ALU.mult).then_inc(lg_step, 1)
                n += 1
                dve.tensor_scalar(T[2], lg_in, 0.0, None, ALU.min).then_inc(lg_step, 1)
                n += 1
                after()
                dve.scalar_tensor_tensor(lg[:].rearrange("p a h -> p (a h)"), T[3], -2.0, T[2], ALU.mult,
                                         ALU.add).then_inc(lg_step, 1)
                n += 1
                after()
                dve.tensor_scalar(nlg[:], lg[:, 1, :], -1.0, None, ALU.mult).then_inc(lg_step, 1)
                for p in range(2):
                    dve.tensor_copy(lgp[DH * p:DH * (p + 1), :, :],
                                    lg[DH * p:DH * (p + 1), :, :].rearrange("p a (i e) -> p a i e", e=2)[:, :, :, p]
                                    ).then_inc(lg_step, 1)

            def rotate(b, layer):
                for tt in range(NT):
                    ps_ = bank[in_bank(b, tt)]
                    dve.wait_ge(*tile_done(b, tt, layer))
                    if b == 1:
                        dve.wait_ge(qk_tp, at(qk_tp, layer, tt + 1))
                    if tt == 0:
                        if b == 1:
                            dve.tensor_copy(kp[:], ps_[:].rearrange("p (h d) -> p h d", h=H)).then_inc(kp_done, 1)
                        dve.tensor_copy(tm[:, 0, :], ps_[:]).then_inc(rope_done, 1)
                        continue
                    n = 3 * (4 * b + tt - 1)
                    src = ps_[:].rearrange("p (h g e f) -> p h g e f", h=H, g=2, e=2)
                    swp = t1[:, 1, :].rearrange("p (h g e f) -> p h g e f", h=H, g=2, e=2)
                    sin = rope[:, 1, tt - 1, :].rearrange("p (g e f) -> p g e f", g=2, e=2)
                    if tt > 1:
                        dve.wait_ge(rope_done, at(rope_done, layer, NT * b + tt))
                    dve.tensor_tensor(t1[:, 0, :].rearrange("p (h d) -> p h d", h=H),
                                      ps_[:].rearrange("p (h d) -> p h d", h=H),
                                      rope[:, 0, tt - 1, :].unsqueeze(1).to_broadcast([P, H, DH]),
                                      ALU.mult).then_inc(rope_part, 1)
                    for e_ in range(2):
                        dve.tensor_tensor(swp[:, :, :, e_, :], src[:, :, :, 1 - e_, :],
                                          sin[:, :, e_, :].unsqueeze(1).to_broadcast([P, H, 2, 16]),
                                          ALU.mult).then_inc(rope_part, 1)
                    dve.wait_ge(rope_part, at(rope_part, layer, n + 3))
                    dve.tensor_tensor(tm[:, tt, :], t1[:, 0, :], t1[:, 1, :], ALU.add).then_inc(rope_done, 1)

            def toe_lower(h, layer):
                dve.wait_ge(toe_lin, at(toe_lin, layer, h + 1))
                dve.scalar_tensor_tensor(toe[:, h % 2, :], dist[:], nlg[:, h:h + 1], toe[:, h % 2, :],
                                         ALU.mult, ALU.min).then_inc(toe_min, 1)

            def toe_diagonal(h, layer):
                dve.wait_ge(toe_exp, at(toe_exp, layer, h + 1))
                dve.tensor_tensor(toe[:, h % 2, 3 * P:4 * P], toe[:, h % 2, 3 * P:4 * P], ident[:],
                                  ALU.add).then_inc(toe_done, 1)

            def decay_queries(a, layer):
                dve.wait_ge(qf_exp, at(qf_exp, layer, a + 1))
                dve.tensor_tensor(qf[:, a % 2, :, :], qf[:, a % 2, :, :],
                                  qT[:, a, P:TOK].unsqueeze(1).to_broadcast([P, 2, LAT]), ALU.mult).then_inc(qf_done, 1)

            def retention(layer):
                dve.wait_ge(kdec_done, at(kdec_done, layer, 1))
                for d in range(2):
                    i_ = dve.tensor_tensor(kd[:, d, :, :], kp[:], kdec[:, d, :].unsqueeze(2).to_broadcast([P, H, DH]),
                                           ALU.mult)
                i_.then_inc(kd_done, 1)
                for h in range(H):
                    if h + 1 < H:
                        toe_lower(h + 1, layer)
                    if h == 0:
                        dve.wait_ge(toe_done, at(toe_done, layer, 1))
                    for j in range(5):
                        u = 5 * h + j
                        n = LAT if j < 4 else P
                        off = 3 * P - P * j if j < 4 else 3 * P
                        dve.wait_ge(ret_s, at(ret_s, layer, u + 1))
                        if u >= 4:
                            dve.wait_ge(ret_av, at(ret_av, layer, u - 3))
                        if j == 0 and h:
                            dve.wait_ge(toe_done, at(toe_done, layer, h + 1))
                        dve.tensor_tensor(pr[:, u % 4, 0:n], bank[RET_BANKS[j]][:, 0:n], toe[:, h % 2, off:off + n],
                                          ALU.mult).then_inc(ret_p, 1)
                    if h + 1 < H:
                        toe_diagonal(h + 1, layer)
                    if h % 2 == 0 and h // 2 + 1 < HP:
                        decay_queries(h // 2 + 1, layer)

            def group_norm(layer):
                for i in range(NT):
                    tt = (i + 1) % NT
                    dve.wait_ge(ret_tp, at(ret_tp, layer, i + 1))
                    o = bank[(tt - 1) % NT][:].rearrange("p (h d) -> p h d", h=H)
                    dve.tensor_reduce(gn[:, 0, tt, :], o, AX.X, ALU.add).then_inc(gn_step, 1)
                    dve.wait_ge(gn_step, at(gn_step, layer, 2 * i + 1))
                    dve.tensor_scalar(gn[:, 1, tt, :], gn[:, 0, tt, :], -1.0 / DH, None, ALU.mult).then_inc(gn_step, 1)
                    dve.wait_ge(gn_step, at(gn_step, layer, 2 * i + 2))
                    dve.tensor_tensor(xc[:, tt, :].rearrange("p (h d) -> p h d", h=H), o,
                                      gn[:, 1, tt, :].unsqueeze(2).to_broadcast([P, H, DH]),
                                      ALU.add).then_inc(gn_read, 1)
                for i in range(NT):
                    tt = (i + 1) % NT
                    dve.wait_ge(gn_sq, at(gn_sq, layer, i + 1))
                    dve.tensor_reduce(gn[:, 2, tt, :], xsq[:, tt, :].rearrange("p (h d) -> p h d", h=H), AX.X,
                                      ALU.add).then_inc(gn_step, 1)
                for i in range(NT):
                    tt = (i + 1) % NT
                    n = 3 * NT + 2 * i
                    dve.wait_ge(gn_std, at(gn_std, layer, i + 1))
                    dve.reciprocal(gn[:, 3, tt, :], gn[:, 3, tt, :]).then_inc(gn_step, 1)
                    dve.wait_ge(gn_step, at(gn_step, layer, n + 1))
                    x3 = xc[:, tt, :].rearrange("p (h d) -> p h d", h=H)
                    dve.tensor_tensor(x3, x3, gn[:, 3, tt, :].unsqueeze(2).to_broadcast([P, H, DH]),
                                      ALU.mult).then_inc(gn_step, 1)
                    dve.wait_ge(gn_step, at(gn_step, layer, n + 2))
                    dve.tensor_tensor(sg[:, tt, :], xc[:, tt, :], sg[:, tt, :], ALU.mult).then_inc(ret_done, 1)

            def post_norm(w, layer):
                gb, y, z = (gb_ffn, y_ffn, zt_ffn) if w else (gb_mix, y_mix, zt)
                dve.wait_ge(gb_done, at(gb_done, layer, 4 * w + 4))
                for tt in range(NT):
                    c, i = (0 if tt == 0 else 1), NT * w + tt
                    dve.wait_ge(post_std, at(post_std, layer, i + 1))
                    dve.reciprocal(rstd[:, tt:tt + 1], std[:, tt:tt + 1]).then_inc(post_rstd, 1)
                    dve.wait_ge(post_rstd, at(post_rstd, layer, i + 1))
                    if tt:
                        dve.wait_ge(x_done, at(x_done, layer, i))
                    src = bank[tt if w else out_bank[1][tt]][:]
                    dve.scalar_tensor_tensor(z[:, 0:W], y[:, tt, :], rstd[:, tt:tt + 1], gb[:, c, 0:W],
                                             ALU.mult, ALU.mult).then_inc(post_y, 1)
                    dve.scalar_tensor_tensor(z[:, W:D], src, rstd[:, tt:tt + 1], gb[:, c, W:D],
                                             ALU.mult, ALU.mult).then_inc(post_y, 1)
                    dve.wait_ge(post_y, at(post_y, layer, 2 * i + 2))
                    dve.tensor_tensor(x[:, tt, :], x[:, tt, :], z[:], ALU.add).then_inc(x_done, 1)

            def first_half(w, layer):
                y = y_ffn if w else y_mix
                for tt in range(NT):
                    dve.wait_ge(y_sq, at(y_sq, layer, 2 * NT * w + tt + 1))
                    dve.tensor_copy(y[:, tt, :], bank[tt][:]).then_inc(y_copied, 1)
                dve.wait_ge(y_sq, at(y_sq, layer, 2 * NT * w + NT))
                dve.tensor_scalar(base[:], ssq[:, 0, :], 1.0 / D, EPS, ALU.mult, ALU.add).then_inc(y_base, 1)

            dve.wait_ge(primed, 1)
            dve.wait_ge(cond_silu, 1)
            for col in range(ADA_FIRST):
                dve.wait_ge(raw_full[col % 4], 16 * (col // 4 + 1))
                if col:
                    dve.wait_ge(ada_part, col)
                ada_products(col, raw[:, col % 4, :], col % 4, 0.0)
            dve.wait_ge(raw_free[(ADA_FIRST - 1) % 4], 1 + LEAD_ROUNDS)
            dve.wait_ge(const_in, 16 * 8)
            with dve.Fori(0, DEPTH) as the_layer:
                layer = stage(dve, the_layer)
                dve.wait_ge(par_in, at(par_in, layer, 96))
                lg_in = dec[:].rearrange("p a h -> p (a h)")
                dve.tensor_scalar(lgt[:, 0, :], lg_in, -1.0, None, ALU.mult).then_inc(lg_step, 1)
                dve.wait_ge(lg_step, at(lg_step, layer, 1))
                dve.tensor_tensor(lgt[:, 1, :], lg_in, lgt[:, 0, :], ALU.max).then_inc(lg_step, 1)
                pre_norm(0, layer)
                for b in range(NB_IN):
                    layer = stage(dve, the_layer)
                    col = ADA_FIRST + 4 * (b + 1)
                    split_lo(4 * (b + 1), layer)
                    split_lo(4 * (b + 1) + 1, layer)
                    ada(col, layer)
                    ada(col + 1, layer)
                    split_lo(4 * (b + 1) + 2, layer)
                    if b < 2:
                        rotate(b, layer)
                    if b == 2:
                        decays(layer)
                    if b == 3:
                        toe_lower(0, layer)
                        toe_diagonal(0, layer)
                        decay_queries(0, layer)
                    split_lo(4 * (b + 1) + 3, layer)
                    if b + 1 < NB_IN:
                        ada(col + 2, layer)
                        ada(col + 3, layer)
                    if b == 3:
                        retention(stage(dve, the_layer))
                        group_norm(stage(dve, the_layer))
                layer = stage(dve, the_layer)
                for tt in range(NT):
                    dve.wait_ge(mix_hi, at(mix_hi, layer, tt + 1))
                    dst = (slice(None), slice(0, HP), slice(tt * P, (tt + 1) * P))
                    dve.tensor_tensor(aT_lo[dst], blk(bank[MIX_BANKS[tt]][:]), aT_hi[dst].bitcast(F32),
                                      ALU.subtract).then_inc(mix_lo, 1)
                layer = stage(dve, the_layer)
                dve.wait_ge(bias_done, at(bias_done, layer, NBIAS))
                dve.wait_ge(kv_out, at(kv_out, layer, 48))
                for i in range(NU + 6):
                    if i < NU:
                        jb, h = UNITS[i]
                        keys, e0 = key_blocks(jb)
                        n = P * len(keys)
                        dve.wait_ge(na_s, at(na_s, layer, i + 1))
                        if i >= 4:
                            dve.wait_ge(na_t, at(na_t, layer, i - 3))
                        if not keys:
                            dve.tensor_reduce(nmax[:, i % 4:i % 4 + 1], bank[NA_BANKS[i % 4]][:, 0:P], AX.X, ALU.max,
                                              negate=True).then_inc(na_m, 1)
                        else:
                            dve.tensor_reduce(cmax[:, i % 4, 0:1], bank[NA_BANKS[i % 4]][:, 0:P], AX.X, ALU.max, negate=True)
                            dve.tensor_tensor_reduce(sp[:, i % 4, P:P + n], bank[NA_BANKS[i % 4]][:, P:P + n],
                                                     bias[:, h, e0:e0 + len(keys), :].rearrange("p e k -> p (e k)"),
                                                     -1.0, BIG, ALU.add, ALU.min, cmax[:, i % 4, 1:2]).then_inc(na_c, 1)
                            dve.wait_ge(na_c, at(na_c, layer, i + 1))
                            dve.tensor_tensor(nmax[:, i % 4:i % 4 + 1], cmax[:, i % 4, 0:1], cmax[:, i % 4, 1:2],
                                              ALU.min).then_inc(na_m, 1)
                    if i in (10, 20):
                        ada(ADA - 3 + i // 10, layer)
                    if i == 30:
                        dve.wait_ge(*freed(stream_ada(ADA - 1), layer))
                        times_gain(4 * KD, C_GF, 1.0).then_inc(mod_done, 1)
                        times_gain(2 * KD, C_PM, 0.0).then_inc(mod_done, 1)
                        times_gain(5 * KD, C_PF, 0.0).then_inc(mod_done, 1)
                    if 1 <= i <= NU:
                        u = i - 1
                        n = P * (1 + len(key_blocks(UNITS[u][0])[0]))
                        sum_, r_ = esum[:, u % 4, 0:1], 2 * u
                        dve.wait_ge(na_e, at(na_e, layer, u + 1))
                        if n > P:
                            dve.tensor_tensor(sum_, sum_, esum[:, u % 4, 1:2], ALU.add).then_inc(na_r, 1)
                            dve.wait_ge(na_r, at(na_r, layer, r_ + 1))
                        else:
                            r_ = NQB * H + u - 1
                        dve.reciprocal(rec[:, u % 4:u % 4 + 1], sum_).then_inc(na_r, 1)
                        dve.wait_ge(na_r, at(na_r, layer, r_ + 2))
                        dve.tensor_scalar(sp[:, u % 4, 0:n], sp[:, u % 4, 0:n], rec[:, u % 4:u % 4 + 1], None,
                                          ALU.mult).then_inc(na_d, 1)
                    if i % 8 == 5 and i >= 8:
                        jb = i // 8 - 1
                        dve.wait_ge(mix_hi, at(mix_hi, layer, NT + jb + 1))
                        src = blk(bank[5 + jb % 2][:])
                        if jb == NQB:
                            dve.tensor_tensor(aT_lo[:, HP:KD, 0:P], src, aT_hi[:, HP:KD, 0:P].bitcast(F32),
                                              ALU.subtract).then_inc(mix_lo, 1)
                        else:
                            for a in range(HP):
                                i_ = dve.tensor_tensor(grid(aT_lo[:, HP + a, P:TOK], jb),
                                                       src[:, a, :].rearrange("p (r c) -> p r c", c=CB),
                                                       grid(aT_hi[:, HP + a, P:TOK].bitcast(F32), jb), ALU.subtract)
                            i_.then_inc(mix_lo, 1)
                layer = stage(dve, the_layer)
                for g in range(W_OUT0 + 4, W_OUT0 + 7):
                    split_lo(g, layer)
                first_half(0, layer)
                split_lo(W_OUT0 + 7, layer)
                post_norm(0, layer)
                layer = stage(dve, the_layer)
                pre_norm(1, layer)
                with dve.Fori(0, KF // 2) as j:
                    for c in range(4):
                        t_ = cv[:, c, :]
                        dve.wait_ge(tap_mid, at(tap_mid, layer, 4 * j + c + 1))
                        for lo, ps_, n in ((0, bank[c], CTX - 1), (CTX, bank[c], TH - CTX), (TH, bank[4 + c], TH - 1)):
                            dve.scalar_tensor_tensor(t_[:, lo + 1:lo + 1 + n], ps_[:, lo % TH:lo % TH + n], tap(0, c, j),
                                                     t_[:, lo + 1:lo + 1 + n], ALU.mult, ALU.add).then_inc(tap_left, 1)
                        dve.wait_ge(tap_left, at(tap_left, layer, 12 * j + 3 * c + 3))
                        for lo, ps_, n in ((1, bank[c], CTX - 1), (CTX + 1, bank[c], TH - CTX - 1), (TH, bank[4 + c], TH)):
                            i_ = dve.scalar_tensor_tensor(t_[:, lo - 1:lo - 1 + n], ps_[:, lo % TH:lo % TH + n], tap(2, c, j),
                                                          t_[:, lo - 1:lo - 1 + n], ALU.mult, ALU.add)
                        i_.then_inc(conv_done, 1)
                        dve.wait_ge(hi_done, at(hi_done, layer, 4 * j + (W_UP0 + 4 + c + 1)))
                        dve.tensor_tensor(w_lo[:, c, :], raw[:, c, :], w_hi[:, c, :].bitcast(F32),
                                          ALU.subtract).then_inc(raw_free[c], 1)
                        if c >= 2:
                            s = c - 2
                            dve.wait_ge(silu_done, at(silu_done, layer, 2 * j + s + 1))
                            dve.tensor_tensor(m[:, bass.ds(2 * j + s, 1), :], cv[:, 2 * s:2 * s + 1, :],
                                              cv[:, 2 * s + 1:2 * s + 2, :], ALU.mult).then_inc(m_done, 1)
                layer = stage(dve, the_layer)
                for gi in range(G_DOWN):
                    if 2 <= gi and gi + 2 < G_DOWN:
                        n, i = divmod(gi + 2, len(DOWN_KT))
                        if i >= 4:
                            ada(ADA_FIRST // 2 * n + i - 4, layer)
                        split_lo(W_DOWN0 + gi + 2, layer)
                    n, i = divmod(gi, len(DOWN_KT))
                    if gi == len(DOWN_KT):
                        first_half(1, layer)
                    for kt in DOWN_KT[i]:
                        q = KF * n + kt
                        dve.wait_ge(mhi_done, at(mhi_done, layer, q + 1))
                        dve.tensor_tensor(m_lo[:, kt % 4, :], m[:, kt, :], m_hi[:, kt % 4, :].bitcast(F32),
                                          ALU.subtract).then_inc(mlo_done, 1)
                post_norm(1, layer)

        @block.tensor
        def _(pe):
            pe.wait_ge(const_in, 16 * 8)

            def mm3(out, lh, ll, rh, rl, start, stop):
                pe.matmul(out, ll, rh, start=start, stop=False)
                pe.matmul(out, lh, rl, start=False, stop=False)
                return pe.matmul(out, lh, rh, start=False, stop=stop)

            def pre_norm_tp(w, layer):
                for k in range(KD):
                    i = KD * w + k
                    if k == 0:
                        pe.wait_ge(diag_done, at(diag_done, layer, NT * w + NT))
                    if k >= 2:
                        pe.wait_ge(norm_mod, at(norm_mod, layer, i - 1))
                    ks = slice(k * P, (k + 1) * P)
                    pe.matmul(bank[CTX_BANK[k % 2]][:, 0:P], x[:, 0, ks], diag[:, 0, :], start=True, stop=True)
                    for tt in range(1, NT):
                        i_ = pe.matmul(bank[5 + k % 2][:, (tt - 1) * P:tt * P], x[:, tt, ks], diag[:, tt, :],
                                       start=True, stop=True)
                    i_.then_inc(norm_tp, 1)

            def qk_transposes(b, tts, layer):
                if tts[0] == 0:
                    if b < 2:
                        pe.wait_ge(rope_done, at(rope_done, layer, NT * (b + 1)))
                    else:
                        pe.wait_ge(in_copied, at(in_copied, layer, NT * (b - 1)))
                for tt in tts:
                    n = NT * qk_blocks.index(b) + tt
                    if tt >= 2:
                        pe.wait_ge(qk_T, at(qk_T, layer, n - 1))
                    out = bank[qk_bank(b, tt)]
                    for a in range(HP):
                        i_ = pe.transpose(out[:, a * P:(a + 1) * P], tm[:, tt, a * P:(a + 1) * P], ident[:])
                    i_.then_inc(qk_tp, 1)

            def bank_free(b, tt, layer):
                if b == 0:
                    if tt == 4:
                        pe.wait_ge(norm_mod, at(norm_mod, layer, KD))
                    return
                if b == 4:
                    if tt == 0:
                        pe.wait_ge(ret_p, at(ret_p, layer, 5 * H))
                    else:
                        pe.wait_ge(gn_read, at(gn_read, layer, tt))
                    return
                if b == 5 and tt < 2:
                    if tt == 0:
                        pe.wait_ge(gn_read, at(gn_read, layer, NT))
                    else:
                        pe.wait_ge(st_done, at(st_done, layer, 1))
                    return
                if tt < 2 and b - 2 in qk_blocks:
                    pe.wait_ge(qk_T, at(qk_T, layer, NT * qk_blocks.index(b - 2) + NT))
                n = NT * b + tt - 7
                if b == 1 and tt < 2:
                    pe.wait_ge(norm_mod, at(norm_mod, layer, KD))
                elif n < 2 * NT:
                    pe.wait_ge(rope_done, at(rope_done, layer, n + 1))
                else:
                    pe.wait_ge(in_copied, at(in_copied, layer, n - 2 * NT + 1))

            def in_granule(b, q, layer):
                g = 4 * b + q
                pe.wait_ge(*freed(stream_of(g), layer))
                for tt in range(NT):
                    if q == 0:
                        bank_free(b, tt, layer)
                    out, tok = bank[in_bank(b, tt)], slice(tt * P, (tt + 1) * P)
                    for kk in range(2):
                        k = 2 * q + kk
                        if b == 0 and tt == 0:
                            pe.wait_ge(norm_lo, at(norm_lo, layer, k + 1))
                        i_ = mm3(out[:], aT_hi[:, k, tok], aT_lo[:, k, tok],
                                 w_hi[:, g % 4, kk * W:(kk + 1) * W], w_lo[:, g % 4, kk * W:(kk + 1) * W],
                                 k == 0, k == KD - 1)
                    if tt == NT - 1:
                        i_.then_inc(w_used, 1)
                    elif q == 3:
                        i_.then_inc(in_done, 1)

            def ret_scores(u, layer):
                h, j = divmod(u, 5)
                hs, a = halves[h]
                part = slice(hs, hs + DH)
                if u >= 5:
                    pe.wait_ge(ret_p, at(ret_p, layer, u - 4))
                if j < 4:
                    i_ = pe.matmul(bank[RET_BANKS[j]][:], kT[part, a, P + P * j:2 * P + P * j], qT[part, a, P:TOK],
                                   start=True, stop=True)
                else:
                    i_ = pe.matmul(bank[RET_BANKS[j]][:, 0:P], kT[part, a, 0:P], qT[part, a, 0:P], start=True, stop=True)
                i_.then_inc(ret_s, 1)

            def ret_values(u, layer):
                h, j = divmod(u, 5)
                hs, a = halves[h]
                part = slice(hs, hs + DH)
                out = bank[a % 2][part, :]
                pe.wait_ge(ret_p, at(ret_p, layer, u + 1))
                if j == 4:
                    pe.matmul(bank[4][part, a * P:(a + 1) * P], vt[:, 0, h, 0:DH], pr[:, u % 4, 0:P], start=True,
                              stop=True).then_inc(ret_av, 1)
                    return
                if j == 0:
                    pe.wait_ge(qf_done, at(qf_done, layer, a + 1))
                    if h % 2 == 0 and a >= 2:
                        pe.wait_ge(ret_oT, at(ret_oT, layer, a - 1))
                i_ = pe.matmul(out, vt[:, 1 + j, h, 0:DH], pr[:, u % 4, :], start=j == 0, stop=j == 3)
                if j == 0:
                    for d in range(2):
                        i_ = pe.matmul(out, st0[part, d, a, :], qf[part, a % 2, d, :], start=False, stop=False)
                i_.then_inc(ret_av, 1)

            def retention(layer):
                pe.wait_ge(par_in, at(par_in, layer, 96))
                pe.wait_ge(in_copied, at(in_copied, layer, 2 * NT))
                for u in range(5 * H + 3):
                    if u < 5 * H:
                        ret_scores(u, layer)
                    if u >= 3:
                        ret_values(u - 3, layer)
                pe.wait_ge(kd_done, at(kd_done, layer, 1))
                pe.wait_ge(ret_p, at(ret_p, layer, 5 * H))
                for d in range(2):
                    for h in range(H):
                        i_ = pe.matmul(bank[5][DH * d:DH * (d + 1), h * DH:(h + 1) * DH], kd[:, d, h, :],
                                       vt[:, 0, h, 0:DH], start=True, stop=True)
                i_.then_inc(st_mm, 1)
                pe.wait_ge(ret_oT, at(ret_oT, layer, HP + 1))
                for i in range(NT):
                    for a in range(HP):
                        i_ = pe.transpose(bank[i][:, a * P:(a + 1) * P], oT[:, a, i * P:(i + 1) * P], ident[:])
                    i_.then_inc(ret_tp, 1)

            def na_scores(u, layer):
                jb, h = UNITS[u]
                hs, a = halves[h]
                part = slice(hs, hs + DH)
                keys, _ = key_blocks(jb)
                if u >= 4:
                    pe.wait_ge(na_e, at(na_e, layer, u - 3))
                out = bank[NA_BANKS[u % 4]]
                if jb == NQB:
                    pe.matmul(out[:, 0:P], qT[part, a, 0:P], kT[part, a, 0:P], start=True, stop=True).then_inc(na_s, 1)
                    return
                q_ = qT[part, a, P + P * jb:2 * P + P * jb]
                pe.matmul(out[:, 0:P], q_, ctx_kT[part, a, :], start=True, stop=True)
                if len(keys) == 3:
                    i_ = pe.matmul(out[:, P:4 * P], q_, kT[part, a, P * jb:P * (jb + 3)], start=True, stop=True)
                else:
                    for n, kb in enumerate(keys):
                        i_ = pe.matmul(out[:, P * (n + 1):P * (n + 2)], q_, kT[part, a, P + P * kb:2 * P + P * kb],
                                       start=True, stop=True)
                i_.then_inc(na_s, 1)

            def na_transposes(u, layer):
                n = 1 + len(key_blocks(UNITS[u][0])[0])
                pe.wait_ge(na_d, at(na_d, layer, u + 1))
                if u >= 2:
                    pe.wait_ge(na_p, at(na_p, layer, u - 1))
                for i in range(n):
                    i_ = pe.transpose(bank[3 + u % 2][:, i * P:(i + 1) * P], sp[:, u % 4, i * P:(i + 1) * P], ident[:])
                i_.then_inc(na_t, 1)

            def na_values(u, layer):
                jb, h = UNITS[u]
                keys, _ = key_blocks(jb)
                hs, a = halves[h]
                pe.wait_ge(na_p, at(na_p, layer, u + 1))
                if h == 0 and jb >= 2:
                    pe.wait_ge(mix_lo, at(mix_lo, layer, NT + jb - 1))
                out = bank[5 + jb % 2][hs:hs + DH, a * P:(a + 1) * P]
                own = vt[:, 0, h, :] if jb == NQB else ctx_v[:, h, :]
                i_ = pe.matmul(out, own, pt[:, u % 2, 0:P], start=True, stop=not keys)
                for n, kb in enumerate(keys):
                    i_ = pe.matmul(out, vt[:, 1 + kb, h, :], pt[:, u % 2, P * (n + 1):P * (n + 2)],
                                   start=False, stop=n == len(keys) - 1)
                i_.then_inc(na_av, 1)

            def gate_rows(w, layer):
                for i in range(4):
                    c, n = i // 2, i % 2
                    for f in range(4):
                        if w and f == 0:
                            pe.wait_ge(gb_done, at(gb_done, layer, i + 1))
                        v_ = mod[:, (5 if w else 2) * KD + 4 * n + f, c:c + 1].to_broadcast([P, P])
                        i_ = pe.matmul(bank[GB_BANKS[i]][:, f * P:(f + 1) * P], v_, ident[:], start=True, stop=True)
                    i_.then_inc(gb_mm, 1)

            with pe.Fori(0, DEPTH) as the_layer:
                layer = stage(pe, the_layer)
                pre_norm_tp(0, layer)
                for b in range(NB_IN):
                    layer = stage(pe, the_layer)
                    in_granule(b, 0, layer)
                    post = b - 1 in qk_blocks
                    if post:
                        qk_transposes(b - 1, (0, 1), layer)
                    in_granule(b, 1, layer)
                    if post:
                        qk_transposes(b - 1, (2, 3), layer)
                    in_granule(b, 2, layer)
                    if post:
                        qk_transposes(b - 1, (4,), layer)
                    in_granule(b, 3, layer)
                    if b == 3:
                        retention(stage(pe, the_layer))
                qk_transposes(6, range(NT), layer)
                layer = stage(pe, the_layer)
                for tt in range(NT):
                    pe.wait_ge(ret_done, at(ret_done, layer, NT))
                    if tt == 2:
                        pe.wait_ge(qk_T, at(qk_T, layer, 4 * NT))
                    if tt == 4:
                        pe.wait_ge(mix_lo, at(mix_lo, layer, 1))
                    for a in range(HP):
                        i_ = pe.transpose(bank[MIX_BANKS[tt]][:, a * P:(a + 1) * P], sg[:, tt, a * P:(a + 1) * P], ident[:])
                    i_.then_inc(mix_tp, 1)
                layer = stage(pe, the_layer)
                pe.wait_ge(qk_T, at(qk_T, layer, 4 * NT))
                pe.wait_ge(v_moved, at(v_moved, layer, PER[v_moved]))
                for i in range(NU + 4):
                    if i < NU:
                        na_scores(i, layer)
                    if i == 3:
                        pe.wait_ge(mix_lo, at(mix_lo, layer, NT))
                    if 3 <= i < NU + 3:
                        na_transposes(i - 3, layer)
                    if i >= 4:
                        na_values(i - 4, layer)
                layer = stage(pe, the_layer)
                pe.wait_ge(mix_lo, at(mix_lo, layer, 2 * NT))
                pe.wait_ge(mod_done, at(mod_done, layer, MOD_ALL))
                gate_rows(0, layer)
                gate_rows(1, layer)
                for q in range(4):
                    g = W_OUT0 + q
                    pe.wait_ge(*freed(stream_of(g), layer))
                    for tt in range(NT):
                        if q == 0 and tt == 4:
                            pe.wait_ge(gb_done, at(gb_done, layer, 8))
                        tok = slice(tt * P, (tt + 1) * P)
                        for kk in range(2):
                            k = 2 * q + kk
                            i_ = mm3(bank[tt][:], aT_hi[:, k, tok], aT_lo[:, k, tok],
                                     w_hi[:, g % 4, kk * W:(kk + 1) * W], w_lo[:, g % 4, kk * W:(kk + 1) * W],
                                     k == 0, k == KD - 1)
                        if tt == NT - 1:
                            i_.then_inc(w_used, 1)
                        elif q == 3:
                            i_.then_inc(y_done, 1)
                for tt in range(NT):
                    tok = slice(tt * P, (tt + 1) * P)
                    if tt >= 3:
                        pe.wait_ge(y_copied, at(y_copied, layer, tt - 2))
                        pe.wait_ge(y_sq, at(y_sq, layer, tt - 2))
                    for q in range(4):
                        g = W_OUT0 + 4 + q
                        if tt == 0:
                            pe.wait_ge(*freed(stream_of(g), layer))
                        for kk in range(2):
                            k = 2 * q + kk
                            i_ = mm3(bank[out_bank[1][tt]][:], aT_hi[:, k, tok], aT_lo[:, k, tok],
                                     w_hi[:, g % 4, kk * W:(kk + 1) * W], w_lo[:, g % 4, kk * W:(kk + 1) * W],
                                     k == 0, k == KD - 1)
                        if tt == NT - 1:
                            i_.then_inc(w_used, 1)
                    if tt < NT - 1:
                        i_.then_inc(y_done, 1)
                layer = stage(pe, the_layer)
                pre_norm_tp(1, layer)
                with pe.Fori(0, KF // 2) as j:
                    pe.wait_ge(norm_mod, at(norm_mod, layer, 2 * KD - 1))
                    for c in range(4):
                        pe.wait_ge(raw_free[c], at(raw_free[c], layer, j + (S_UP0 // 4 + 1)))
                        pe.wait_ge(conv_done, at(conv_done, layer, 4 * j + c - 3))
                        for k in range(KD):
                            if c == 0:
                                pe.wait_ge(norm_lo, at(norm_lo, layer, KD + k + 1))
                            wh, wl = w_hi[:, c, k * P:(k + 1) * P], w_lo[:, c, k * P:(k + 1) * P]
                            outs = ((bank[c][:, 0:TH], slice(0, TH)), (bank[4 + c][:, 0:TH], slice(TH, TOK)))
                            for out, tok in outs:
                                pe.matmul(out, wl, aT_hi[:, k, tok], start=k == 0, stop=False)
                            for out, tok in outs:
                                pe.matmul(out, wh, aT_lo[:, k, tok], start=False, stop=False)
                            for out, tok in outs:
                                i_ = pe.matmul(out, wh, aT_hi[:, k, tok], start=False, stop=k == KD - 1)
                        i_.then_inc(w_used, 1)
                pe.wait_ge(conv_done, at(conv_done, layer, G_UP))
                layer = stage(pe, the_layer)
                for n in range(2):
                    by_tile = 3 * n

                    def down_ready(i):
                        s = stream_down(i)
                        pe.wait_ge(raw_free[s % 4], at(raw_free[s % 4], layer, S_HALF // 4 * n + (s // 4 + 1)))
                        pe.wait_ge(mlo_done, at(mlo_done, layer, KF * n + (DOWN_KT[i][-1] + 1)))

                    def down_tile(i, tt):
                        for kk, kt in enumerate(DOWN_KT[i]):
                            q = kt % 4
                            tok = slice(tt * P, (tt + 1) * P)
                            i_ = mm3(bank[tt][:], m_hi[:, q, tok], m_lo[:, q, tok],
                                     w_hi[:, i % 4, kk * W:(kk + 1) * W], w_lo[:, i % 4, kk * W:(kk + 1) * W],
                                     kt == 0, kt == KF - 1)
                        if tt == NT - 1:
                            i_.then_inc(w_used, 1)
                        elif i == len(DOWN_KT) - 1:
                            i_.then_inc(y_done, 1)

                    for i in range(len(DOWN_KT) - by_tile):
                        down_ready(i)
                        for tt in range(NT):
                            if i == 0:
                                pe.wait_ge(y_copied, at(y_copied, layer, NT * n + (tt + 1)))
                                pe.wait_ge(y_sq, at(y_sq, layer, NT * n + (NT + tt + 1)))
                            down_tile(i, tt)
                    for tt in range(NT):
                        for i in range(len(DOWN_KT) - by_tile, len(DOWN_KT)):
                            if tt == 0:
                                down_ready(i)
                            down_tile(i, tt)


def bind(nc, arrays, outs):
    a = {n: nc.dram_tensor("in_" + n, v.shape, mybir.dt.from_np(v.dtype), kind="ExternalInput").ap() for n, v in arrays.items()}
    for n, shape in outs.items():
        a[n] = nc.dram_tensor("out_" + n, shape, F32, kind="ExternalOutput").ap()
    return a


def constants():
    f = np.float32
    inv = np.power(f(10000.0), -np.arange(0, 32, 2, dtype=f) / f(32))
    pos = np.arange(LAT)
    cos = np.zeros((LAT, 2, 2, 16), f)
    sin = np.zeros((LAT, 2, 2, 16), f)
    for g, p in enumerate((pos // GRID_W, pos % GRID_W)):
        ang = p[:, None].astype(f) * inv[None, :]
        cos[:, g] = np.cos(ang)[:, None]
        sin[:, g, 0], sin[:, g, 1] = -np.sin(ang), np.sin(ang)
    rope = np.stack([cos.reshape(LAT, DH), sin.reshape(LAT, DH)])
    rope = rope.reshape(2, NT - 1, P, DH).transpose(2, 0, 1, 3)
    p = np.arange(P)
    dist = np.arange(DIST)[None, :] - 3 * P - p[:, None]
    i = np.arange(LAT)
    qpos = np.broadcast_to(np.stack([i + 1, LAT - i])[None], (P, 2, LAT))
    kpos = np.stack([P - 1 - p, p], 1)
    c, k = p[:, None] % CB, np.arange(CB)[None, :]
    half = CB // 2
    ok = np.stack([k < c + half,
                   k - CB >= c - half,
                   (k >= c - half) & (k < c + half),
                   k + CB < c + half,
                   k >= c - half], 1)
    masks = np.where(ok, 0.0, NEG)
    return {n: np.ascontiguousarray(v, dtype=np.float16 if n in ("dist", "qpos") else f) for n, v in
            dict(ident=np.eye(P), rope=rope, dist=dist, qpos=qpos, kpos=kpos, masks=masks).items()}


def layout(inp):
    a = constants()
    f = np.float32
    a["xp"], a["xs"] = inp["x_prompt"][0], inp["x_sample"][0]
    a["cond"] = np.stack([inp["c_ctx"], inp["c"][0]]).reshape(1, 2 * D)
    par = np.zeros((DEPTH, NPAR, P), f)
    lead = np.zeros((ADA_FIRST, P, 1024), f)
    stream = np.zeros((DEPTH, GS, P, 1024), f)
    for l in range(DEPTH):
        par[l] = np.concatenate([np.asarray(inp[n][l]).reshape(-1, P) for n in
                                 ("conv_w", "conv_b", "ada_b", "g_pre_mix", "g_pre_ffn", "g_post_mix", "g_post_ffn")])
        cols = lambda w, c: w[:, c:c + P].reshape(KD, P, P).transpose(1, 0, 2).reshape(P, 1024)
        rows = lambda w, r, n, c: w[r * P:(r + n) * P, c:c + W].reshape(n, P, W).transpose(1, 0, 2).reshape(P, n * W)
        for j in range(ADA):
            if j >= ADA_FIRST:
                stream[l, stream_ada(j)] = inp["ada_w"][l][:, j * P:(j + 1) * P].T
            elif l + 1 < DEPTH:
                stream[l, stream_ada(j)] = inp["ada_w"][l + 1][:, j * P:(j + 1) * P].T
            if j < ADA_FIRST and l == 0:
                lead[j] = inp["ada_w"][0][:, j * P:(j + 1) * P].T
        for b in range(NB_IN):
            for q in range(4):
                stream[l, stream_in(b, q)] = rows(inp["w_in"][l], 2 * q, 2, W_IN_COL[b] * W)
        for n in range(2):
            for q in range(4):
                stream[l, stream_out(4 * n + q)] = rows(inp["w_out"][l], 2 * q, 2, n * W)
            for i, kts in enumerate(DOWN_KT):
                stream[l, stream_down(len(DOWN_KT) * n + i), :, 0:len(kts) * W] = rows(inp["w_down"][l], kts[0], len(kts), n * W)
        for j in range(KF):
            for g in range(2):
                stream[l, S_UP0 + 2 * j + g] = cols(inp["w_up"][l], (g * KF + j) * P)
    a["par"] = par.transpose(0, 2, 1)
    rounds = np.concatenate([lead, stream.reshape(-1, P, 1024)])
    a["stream"] = rounds.reshape(LEAD_ROUNDS + DEPTH * ROUNDS, SLOTS, P, 1024).transpose(1, 0, 2, 3)
    a["dec_f"], a["dec_b"] = inp["ret_decay_fwd"], inp["ret_decay_bwd"]
    st = np.stack([inp["state_ret_fwd"][0], inp["state_ret_bwd"][0]])
    a["st0"] = st.reshape(2, DEPTH, HP, 2, DH, DH).transpose(1, 3, 4, 0, 2, 5).reshape(DEPTH, P, 2 * HP * DH)
    a["ctx_kT"] = np.asarray(inp["cache_na_k"])[0].reshape(DEPTH, P, HP, P).transpose(0, 3, 2, 1).reshape(DEPTH, P, HP * P)
    a["ctx_v"] = inp["cache_na_v"][0]
    pad = np.zeros((DEPTH, H, 15, 63), f)
    pad[:, :, :, CB:CB + 31] = inp["na_rpb"]
    win = np.zeros((DEPTH, P, H, ROWS, 3 * CB), f)
    for r in range(ROWS):
        for c in range(CB):
            win[:, r * CB + c] = pad[:, :, 7 - r:15 - r, 15 - c:63 - c]
    a["bias"] = win.reshape(DEPTH, P, H * ROWS * 3 * CB)
    return {n: np.ascontiguousarray(v) for n, v in a.items()}


OUTS = {"yp": (CTX, D), "ys": (LAT, D), "nk": (DEPTH, P, W), "nv": (DEPTH, P, W), "st": (DEPTH, P, H * DH)}


def kernel(**inputs):
    import concourse.bacc as bacc
    from concourse.bass_utils import run_bass_kernel_spmd

    nc = bacc.Bacc("TRN2", target_bir_lowering=False, num_devices=1, dynamic_dma_scratch_size=1024)
    arrays = layout({n: np.asarray(v) for n, v in inputs.items()})
    build(nc, bind(nc, arrays, OUTS))
    r = run_bass_kernel_spmd(nc, [{"in_" + n: v for n, v in arrays.items()}], core_ids=[0]).results[0]
    r = {n: r["out_" + n] for n in OUTS}
    st = r["st"].reshape(DEPTH, 2, DH, H, DH).transpose(1, 0, 3, 2, 4)
    nk, nv = (r[n].reshape(1, DEPTH, P, H, DH) for n in ("nk", "nv"))
    return r["yp"][None], r["ys"][None], nk, nv, st[0][None], st[1][None]
```
